# Optimizing a Trainium2 kernel written in Bass

```python
import jax, jax.numpy as jnp
from jax import lax
import numpy as np
import math

D_MODEL = 1024
BATCH = 1
SEQ = 1024
DEPTH = 2

GRID_W = 64
CTX_LEN = 256
BRANCH = 256
MIX_WIDTH = 4 * BRANCH
CONV_K = 3
ATT_HEADS = 4
ATT_KV_HEADS = 2
HEAD_DIM = 64
ROPE_THETA = 10000.0
Q_BLOCK = 128
HG_HEADS = 4
HG_DK = BRANCH // HG_HEADS
HG_DV = BRANCH // HG_HEADS
HG_CHUNK = 64
FN_GROUPS = 4
FN_DIM = BRANCH // FN_GROUPS
EPS = 1e-6

IN_SPLITS = (256, 256, 256, 256,
             256, 128, 128, 256,
             256, 256, 256, 256, 256,
             256, 256)
IN_COLS = 3584


def rms_norm(x, g):
    xf = x.astype(jnp.float32)
    y = xf * lax.rsqrt(jnp.mean(xf * xf, axis=-1, keepdims=True) + EPS)
    return (y * g.astype(jnp.float32)).astype(x.dtype)

def split_cols(t):
    points = [int(p) for p in np.cumsum(IN_SPLITS)[:-1]]
    return jnp.split(t, points, axis=-1)

def axial_rope_tables(rows, dtype):
    r, cidx = jnp.meshgrid(jnp.arange(rows), jnp.arange(GRID_W), indexing="ij")
    r = r.reshape(-1).astype(jnp.float32)
    cidx = cidx.reshape(-1).astype(jnp.float32)
    n_pairs = HEAD_DIM // 4
    freqs = ROPE_THETA ** (-jnp.arange(n_pairs, dtype=jnp.float32) / n_pairs)
    ang = jnp.concatenate([r[:, None] * freqs, cidx[:, None] * freqs], axis=-1)
    return jnp.cos(ang).astype(dtype), jnp.sin(ang).astype(dtype)

def apply_rope(x, cos, sin):
    x1, x2 = x[..., 0::2], x[..., 1::2]
    return jnp.stack([x1 * cos - x2 * sin, x1 * sin + x2 * cos], axis=-1).reshape(x.shape)

def to_heads(t, n_heads):
    b, n, _ = t.shape
    return t.reshape(b, n, n_heads, -1).transpose(0, 2, 1, 3)

def from_heads(t):
    b, h, n, d = t.shape
    return t.transpose(0, 2, 1, 3).reshape(b, n, h * d)

def short_conv(u, w):
    up = jnp.pad(u, ((0, 0), (1, 1), (0, 0)))
    return up[:, :-2] * w[0] + up[:, 1:-1] * w[1] + up[:, 2:] * w[2]

def attend(qb, k, v):
    s = jnp.einsum("bhgqd,bhkd->bhgqk", qb, k).astype(jnp.float32) * (HEAD_DIM ** -0.5)
    p = jax.nn.softmax(s, axis=-1).astype(v.dtype)
    return jnp.einsum("bhgqk,bhkd->bhgqd", p, v)

def gqa_branch(q_l, k_l, v_l, q_c, k_c, v_c, q_g, k_g, cos, sin, need_ctx):
    b, n, _ = q_l.shape
    g = ATT_HEADS // ATT_KV_HEADS
    ql = apply_rope(rms_norm(to_heads(q_l, ATT_HEADS), q_g), cos, sin)
    kl = apply_rope(rms_norm(to_heads(k_l, ATT_KV_HEADS), k_g), cos, sin)
    vl = to_heads(v_l, ATT_KV_HEADS)
    kc = rms_norm(to_heads(k_c, ATT_KV_HEADS), k_g)
    vc = to_heads(v_c, ATT_KV_HEADS)
    k_all = jnp.concatenate([kl, kc], axis=2)
    v_all = jnp.concatenate([vl, vc], axis=2)
    nb = n // Q_BLOCK
    qb = ql.reshape(b, ATT_KV_HEADS, g, nb, Q_BLOCK, HEAD_DIM).transpose(3, 0, 1, 2, 4, 5)
    ob = lax.map(lambda blk: attend(blk, k_all, v_all), qb)
    o_lat = ob.transpose(1, 0, 4, 2, 3, 5).reshape(b, n, ATT_HEADS * HEAD_DIM)
    o_ctx = None
    if need_ctx:
        nc = q_c.shape[1]
        qc = rms_norm(to_heads(q_c, ATT_HEADS), q_g).reshape(b, ATT_KV_HEADS, g, nc, HEAD_DIM)
        oc = attend(qc, kc, vc)
        o_ctx = oc.transpose(0, 3, 1, 2, 4).reshape(b, nc, ATT_HEADS * HEAD_DIM)
    return o_lat, o_ctx

def hgrn_lower_bounds(lb_param):
    p = jax.nn.softmax(lb_param.astype(jnp.float32), axis=1)
    cs = jnp.cumsum(p, axis=1)
    return cs - cs[:, :1]

def hgrn_gates(fx, lb):
    fx = fx.astype(jnp.float32)
    log_f = jnp.logaddexp(jnp.log(lb), jnp.log1p(-lb) + jax.nn.log_sigmoid(fx))
    k = (1.0 - lb) * jax.nn.sigmoid(-fx)
    return log_f, k

def hgrn_scan(q, k, v, log_f, s0, with_output):
    b, h, t, _ = q.shape
    n = t // HG_CHUNK

    def chunks(a):
        return a.astype(jnp.float32).reshape(b, h, n, HG_CHUNK, a.shape[-1]).transpose(2, 0, 1, 3, 4)

    causal = jnp.tril(jnp.ones((HG_CHUNK, HG_CHUNK), dtype=bool))[:, :, None]

    def step(state, inp):
        qc, kc, vc, lf = inp
        a = jnp.cumsum(lf, axis=2)
        a_last = a[:, :, -1:, :]
        s_new = jnp.exp(a_last)[:, :, 0, :, None] * state + jnp.einsum(
            "bhsk,bhsv->bhkv", kc * jnp.exp(a_last - a), vc)
        if not with_output:
            return s_new, None
        inter = jnp.einsum("bhtk,bhkv->bhtv", qc * jnp.exp(a), state)
        diff = a[:, :, :, None, :] - a[:, :, None, :, :]
        dec = jnp.exp(jnp.where(causal, diff, -jnp.inf))
        scores = jnp.einsum("bhtk,bhsk,bhtsk->bhts", qc, kc, dec)
        intra = jnp.einsum("bhts,bhsv->bhtv", scores, vc)
        return s_new, inter + intra

    s_fin, out = lax.scan(step, s0, (chunks(q), chunks(k), chunks(v), chunks(log_f)))
    if with_output:
        out = out.transpose(1, 2, 0, 3, 4).reshape(b, h, t, v.shape[-1])
    return s_fin, out

def hgrn_branch(q_l, ff_l, fb_l, i_l, q_c, ff_c, fb_c, i_c, lb, hg_g, need_ctx):
    b = q_l.shape[0]
    ql = to_heads(jax.nn.silu(q_l), HG_HEADS)
    il = to_heads(i_l, HG_HEADS)
    qc = to_heads(jax.nn.silu(q_c), HG_HEADS)
    ic = to_heads(i_c, HG_HEADS)
    o_lat, o_ctx = 0.0, 0.0
    for d, (f_l, f_c) in enumerate(((ff_l, ff_c), (fb_l, fb_c))):
        flip = (lambda a: a[:, :, ::-1]) if d == 1 else (lambda a: a)
        logf_l, k_l = hgrn_gates(f_l, lb[d])
        logf_c, k_c = hgrn_gates(f_c, lb[d])
        s0 = jnp.zeros((b, HG_HEADS, HG_DK, HG_DV), jnp.float32)
        s_ctx, oc = hgrn_scan(flip(qc), flip(to_heads(k_c, HG_HEADS)), flip(ic),
                              flip(to_heads(logf_c, HG_HEADS)), s0, need_ctx)
        _, ol = hgrn_scan(flip(ql), flip(to_heads(k_l, HG_HEADS)), flip(il),
                          flip(to_heads(logf_l, HG_HEADS)), s_ctx, True)
        o_lat = o_lat + flip(ol)
        if need_ctx:
            o_ctx = o_ctx + flip(oc)
    gain = hg_g.reshape(HG_HEADS, 1, HG_DV)
    out_l = from_heads(rms_norm(o_lat, gain)).astype(q_l.dtype)
    out_c = from_heads(rms_norm(o_ctx, gain)).astype(q_l.dtype) if need_ctx else None
    return out_l, out_c

def fourier_mix(u):
    b, t, _ = u.shape
    uf = u.astype(jnp.float32).reshape(b, t, FN_GROUPS, FN_DIM)
    y = jnp.fft.fft2(uf, axes=(1, 3), norm="ortho").real
    return y.reshape(b, t, BRANCH).astype(u.dtype)

def mix_stream(parts, conv_w):
    cb, cc, cv, cz, _, _, _, az, _, _, _, _, hz, fu, fz = parts
    y_conv = cb * short_conv(cc * cv, conv_w) * jax.nn.silu(cz)
    y_four = fourier_mix(fu) * jax.nn.silu(fz)
    return y_conv, y_four, jax.nn.silu(az), jax.nn.silu(hz)

def hybrid_layer(h, hc, c_act, cc_act, norm_g, w_mod, b_mod, w_in, conv_w, q_g, k_g, lb, hg_g,
                 w_out, cos, sin, need_ctx):
    shift, scale, gate = jnp.split((c_act @ w_mod + b_mod)[:, None, :], 3, axis=-1)
    shift_c, scale_c, gate_c = jnp.split(cc_act @ w_mod + b_mod, 3, axis=-1)
    lat = split_cols((rms_norm(h, norm_g) * (1.0 + scale) + shift) @ w_in)
    cx = split_cols((rms_norm(hc, norm_g) * (1.0 + scale_c) + shift_c) @ w_in)

    att_l, att_c = gqa_branch(lat[4], lat[5], lat[6], cx[4], cx[5], cx[6], q_g, k_g, cos, sin, need_ctx)
    hg_l, hg_c = hgrn_branch(lat[8], lat[9], lat[10], lat[11], cx[8], cx[9], cx[10], cx[11],
                             lb, hg_g, need_ctx)

    y_conv, y_four, g_att, g_hg = mix_stream(lat, conv_w)
    y = jnp.concatenate([y_conv, att_l * g_att, hg_l * g_hg, y_four], axis=-1) @ w_out
    h_new = h + gate * y
    hc_new = None
    if need_ctx:
        yc_conv, yc_four, gc_att, gc_hg = mix_stream(cx, conv_w)
        yc = jnp.concatenate([yc_conv, att_c * gc_att, hg_c * gc_hg, yc_four], axis=-1) @ w_out
        hc_new = hc + gate_c * yc
    return h_new, hc_new

def first_inputs(seed: int = 0) -> dict:
    key = jax.random.key(seed)
    ks = jax.random.split(key, 16)
    f32 = jnp.float32
    nrm = lambda k, shape: jax.random.normal(k, shape, f32)
    return {
        "x": nrm(ks[0], (BATCH, SEQ, D_MODEL)),
        "c": nrm(ks[1], (BATCH, D_MODEL)),
        "ctx": nrm(ks[2], (BATCH, CTX_LEN, D_MODEL)),
        "c_ctx": nrm(ks[3], (D_MODEL,)),
        "norm_g": 1.0 + 0.1 * nrm(ks[4], (DEPTH, D_MODEL)),
        "w_mod": nrm(ks[5], (DEPTH, D_MODEL, 3 * D_MODEL)) * (0.5 * D_MODEL ** -0.5),
        "b_mod": 0.02 * nrm(ks[6], (DEPTH, 3 * D_MODEL)),
        "w_in": nrm(ks[7], (DEPTH, D_MODEL, IN_COLS)) * (D_MODEL ** -0.5),
        "conv_w": nrm(ks[8], (DEPTH, CONV_K, BRANCH)) * (CONV_K ** -0.5),
        "q_norm_g": 1.0 + 0.1 * nrm(ks[9], (DEPTH, HEAD_DIM)),
        "k_norm_g": 1.0 + 0.1 * nrm(ks[10], (DEPTH, HEAD_DIM)),
        "hgrn_lb": nrm(ks[11], (2, DEPTH, BRANCH)),
        "hgrn_norm_g": 1.0 + 0.1 * nrm(ks[12], (DEPTH, BRANCH)),
        "w_out": nrm(ks[13], (DEPTH, MIX_WIDTH, D_MODEL)) * (MIX_WIDTH ** -0.5),
        "final_g": 1.0 + 0.1 * nrm(ks[14], (D_MODEL,)),
    }

def first_block(x, c, ctx, c_ctx, norm_g, w_mod, b_mod, w_in, conv_w, q_norm_g, k_norm_g,
              hgrn_lb, hgrn_norm_g, w_out, final_g):
    rows = x.shape[1] // GRID_W
    cos, sin = axial_rope_tables(rows, x.dtype)
    lb_all = hgrn_lower_bounds(hgrn_lb)
    c_act = jax.nn.silu(c)
    cc_act = jax.nn.silu(c_ctx)
    h, hc = x, ctx
    for layer in range(DEPTH):
        h, hc = hybrid_layer(h, hc, c_act, cc_act, norm_g[layer], w_mod[layer], b_mod[layer],
                             w_in[layer], conv_w[layer], q_norm_g[layer], k_norm_g[layer],
                             lb_all[:, layer], hgrn_norm_g[layer], w_out[layer], cos, sin,
                             need_ctx=layer < DEPTH - 1)
    return rms_norm(h, final_g)


DEPTH_2 = 1


N_ATTN_HEADS = 16
QK_NOPE_DIM = 64
QK_ROPE_DIM = 32
V_HEAD_DIM = 64
Q_LORA_RANK = 384
KV_LORA_RANK = 256
ATTN_SCALE = (QK_NOPE_DIM + QK_ROPE_DIM) ** -0.5

N_SSD_HEADS = 16
SSD_HEAD_DIM = 64
SSD_GROUPS = 2
HEADS_PER_GROUP = N_SSD_HEADS // SSD_GROUPS
SSD_STATE = 128
SSD_CONV = 5
SSD_CHUNK = 128
D_INNER = N_SSD_HEADS * SSD_HEAD_DIM
GN = SSD_GROUPS * SSD_STATE
XBC_WIDTH = D_INNER + 2 * GN

ATTN_WIDTH = N_ATTN_HEADS * V_HEAD_DIM
MIX_WIDTH_2 = ATTN_WIDTH + D_INNER

D_FF = 2816
FFN_CONV = 3

N_MOD = 6

IN_SPLITS_2 = (Q_LORA_RANK, KV_LORA_RANK, QK_ROPE_DIM, D_INNER, XBC_WIDTH, 2 * N_SSD_HEADS)
IN_WIDTH = sum(IN_SPLITS_2)
IN_OFFSETS = tuple(int(o) for o in np.cumsum(IN_SPLITS_2)[:-1])


def rms_norm_2(x, w):
    xf = x.astype(jnp.float32)
    y = xf * lax.rsqrt(jnp.mean(xf * xf, axis=-1, keepdims=True) + EPS)
    return (y * w.astype(jnp.float32)).astype(x.dtype)

def modulate(h, shift, scale):
    return h * (1 + scale) + shift

def in_split(h):
    return jnp.split(h, IN_OFFSETS, axis=-1)

def depthwise_conv(x, w, b):
    k = w.shape[0]
    out = lax.conv_general_dilated(
        x, w[:, None, :].astype(x.dtype), window_strides=(1,), padding=((k // 2, k // 2),),
        dimension_numbers=("NWC", "WIO", "NWC"), feature_group_count=x.shape[-1])
    return out + b

def axial_rope_tables_2(seq_len):
    n_rows = seq_len // GRID_W
    row = jnp.repeat(jnp.arange(n_rows), GRID_W).astype(jnp.float32)
    col = jnp.tile(jnp.arange(GRID_W), n_rows).astype(jnp.float32)
    axis_dim = QK_ROPE_DIM // 2
    inv_freq = ROPE_THETA ** (-jnp.arange(0, axis_dim, 2, dtype=jnp.float32) / axis_dim)
    ang_r = row[:, None] * inv_freq
    ang_c = col[:, None] * inv_freq
    ang = jnp.concatenate([ang_r, ang_r, ang_c, ang_c], axis=-1)
    return jnp.cos(ang), jnp.sin(ang)

def rotate_half_axial(x):
    def rh(t):
        a, b = jnp.split(t, 2, axis=-1)
        return jnp.concatenate([-b, a], axis=-1)
    xr, xc = jnp.split(x, 2, axis=-1)
    return jnp.concatenate([rh(xr), rh(xc)], axis=-1)

def apply_rope_2(x, cos, sin):
    xf = x.astype(jnp.float32)
    return (xf * cos + rotate_half_axial(xf) * sin).astype(x.dtype)

def mla_queries(cq, q_norm_w, w_q_up):
    b, l, _ = cq.shape
    q = (rms_norm_2(cq, q_norm_w) @ w_q_up).reshape(b, l, N_ATTN_HEADS, QK_NOPE_DIM + QK_ROPE_DIM)
    return q[..., :QK_NOPE_DIM], q[..., QK_NOPE_DIM:]

def mla_keys_values(ckv, kv_norm_w, w_kv_up):
    b, l, _ = ckv.shape
    kv = (rms_norm_2(ckv, kv_norm_w) @ w_kv_up).reshape(b, l, N_ATTN_HEADS, QK_NOPE_DIM + V_HEAD_DIM)
    return kv[..., :QK_NOPE_DIM], kv[..., QK_NOPE_DIM:]

def attend_2(q_nope, q_rope, k_nope, k_rope, v):
    s = (jnp.einsum("bqhd,bkhd->bhqk", q_nope, k_nope)
         + jnp.einsum("bqhr,bkr->bhqk", q_rope, k_rope)) * ATTN_SCALE
    p = jax.nn.softmax(s.astype(jnp.float32), axis=-1).astype(v.dtype)
    return jnp.einsum("bhqk,bkhd->bqhd", p, v)

def latent_attention(q_nope, q_rope, k_nope, k_rope, v):
    b, s, h, _ = q_nope.shape
    nb = s // Q_BLOCK

    def to_blocks(t):
        return jnp.moveaxis(t.reshape(b, nb, Q_BLOCK, *t.shape[2:]), 1, 0)

    out = lax.map(lambda qb: attend_2(qb[0], qb[1], k_nope, k_rope, v),
                  (to_blocks(q_nope), to_blocks(q_rope)))
    return jnp.moveaxis(out, 0, 1).reshape(b, s, h * V_HEAD_DIM)

def ssd_prepare(xbc, dt_raw, conv_w, conv_b, dt_bias):
    b, l, _ = xbc.shape
    xbc = jax.nn.silu(depthwise_conv(xbc, conv_w, conv_b))
    xs, bm, cm = jnp.split(xbc, [D_INNER, D_INNER + GN], axis=-1)
    xs = xs.reshape(b, l, SSD_GROUPS, HEADS_PER_GROUP, SSD_HEAD_DIM)
    bm = bm.reshape(b, l, SSD_GROUPS, SSD_STATE)
    cm = cm.reshape(b, l, SSD_GROUPS, SSD_STATE)
    dt = jax.nn.softplus(dt_raw.astype(jnp.float32).reshape(b, l, 2, SSD_GROUPS, HEADS_PER_GROUP)
                         + dt_bias.astype(jnp.float32).reshape(2, SSD_GROUPS, HEADS_PER_GROUP))
    return xs, bm, cm, dt

def segment_decay(cum):
    n = cum.shape[-1]
    diff = cum[..., :, None] - cum[..., None, :]
    mask = jnp.tril(jnp.ones((n, n), dtype=bool))
    return jnp.exp(jnp.where(mask, diff, -jnp.inf))

def ssd_states(xh, dt, A, bm, cm, init_state):
    b, l, g, e, p = xh.shape
    nc = l // SSD_CHUNK
    xd = (xh * dt[..., None]).reshape(b, nc, SSD_CHUNK, g, e, p)
    a_cum = jnp.cumsum(jnp.moveaxis((dt * A).reshape(b, nc, SSD_CHUNK, g, e), 2, -1), axis=-1)
    bc = bm.reshape(b, nc, SSD_CHUNK, g, -1)
    cc = cm.reshape(b, nc, SSD_CHUNK, g, -1)
    decay_to_end = jnp.exp(a_cum[..., -1:] - a_cum)
    chunk_states = jnp.einsum("bclgn,bcgel,bclgep->bcgepn", bc, decay_to_end, xd)
    states = jnp.concatenate([init_state[:, None], chunk_states], axis=1)
    chunk_cum = jnp.cumsum(jnp.pad(a_cum[..., -1], ((0, 0), (1, 0), (0, 0), (0, 0))), axis=1)
    decay_chunks = segment_decay(jnp.moveaxis(chunk_cum, 1, -1))
    states = jnp.einsum("bgezc,bcgepn->bzgepn", decay_chunks, states)
    return (xd, a_cum, bc, cc), states[:, :-1], states[:, -1]

def ssd_output(pieces, entering_states):
    xd, a_cum, bc, cc = pieces
    within = segment_decay(a_cum)
    cb = jnp.einsum("bclgn,bcsgn->bcgls", cc, bc)
    y_diag = jnp.einsum("bcgls,bcgels,bcsgep->bclgep", cb, within, xd)
    y_off = jnp.einsum("bclgn,bcgepn,bcgel->bclgep", cc, entering_states, jnp.exp(a_cum))
    b, nc, q, g, e, p = y_diag.shape
    return (y_diag + y_off).reshape(b, nc * q, g, e, p)

def ssd_finish(y, xs, z, d_skip, norm_w):
    b, l = y.shape[:2]
    y = y + d_skip.reshape(SSD_GROUPS, HEADS_PER_GROUP, 1) * xs
    y = y.reshape(b, l, D_INNER).astype(z.dtype)
    return rms_norm_2(y * jax.nn.silu(z), norm_w)

def conv_glu(h, w_up, conv_w, conv_b, w_down):
    gate, val = jnp.split(h @ w_up, 2, axis=-1)
    gate = depthwise_conv(gate, conv_w, conv_b)
    return (jax.nn.gelu(gate, approximate=False) * val) @ w_down

def second_inputs(seed: int = 0) -> dict:
    key = jax.random.key(seed)
    ks = jax.random.split(key, 32)
    f32 = jnp.float32
    L = DEPTH_2

    def dense(k, shape, fan_in):
        return jax.random.normal(k, shape, f32) * fan_in ** -0.5

    def gain(k, shape):
        return 1.0 + 0.1 * jax.random.normal(k, shape, f32)

    def bias(k, shape):
        return 0.02 * jax.random.normal(k, shape, f32)

    dt0 = jnp.exp(jax.random.uniform(ks[15], (L, 2, N_SSD_HEADS), f32, math.log(1e-3), math.log(1e-1)))
    return {
        "x": jax.random.normal(ks[0], (BATCH, SEQ, D_MODEL), f32),
        "c": jax.random.normal(ks[1], (BATCH, D_MODEL), f32),
        "ctx": jax.random.normal(ks[2], (BATCH, CTX_LEN, D_MODEL), f32),
        "c_ctx": jax.random.normal(ks[3], (D_MODEL,), f32),
        "w_mod": dense(ks[4], (L, D_MODEL, N_MOD * D_MODEL), D_MODEL),
        "b_mod": bias(ks[5], (L, N_MOD * D_MODEL)),
        "mix_pre_norm": gain(ks[6], (L, D_MODEL)),
        "mix_post_norm": gain(ks[7], (L, D_MODEL)),
        "w_in": dense(ks[8], (L, D_MODEL, IN_WIDTH), D_MODEL),
        "q_norm": gain(ks[9], (L, Q_LORA_RANK)),
        "w_q_up": dense(ks[10], (L, Q_LORA_RANK, N_ATTN_HEADS * (QK_NOPE_DIM + QK_ROPE_DIM)), Q_LORA_RANK),
        "kv_norm": gain(ks[11], (L, KV_LORA_RANK)),
        "w_kv_up": dense(ks[12], (L, KV_LORA_RANK, N_ATTN_HEADS * (QK_NOPE_DIM + V_HEAD_DIM)), KV_LORA_RANK),
        "ssd_conv_w": dense(ks[13], (L, SSD_CONV, XBC_WIDTH), SSD_CONV),
        "ssd_conv_b": bias(ks[14], (L, XBC_WIDTH)),
        "ssd_a_log": jnp.log(jax.random.uniform(ks[16], (L, 2, N_SSD_HEADS), f32, 1.0, 16.0)),
        "ssd_dt_bias": dt0 + jnp.log(-jnp.expm1(-dt0)),
        "ssd_d": gain(ks[17], (L, N_SSD_HEADS)),
        "ssd_norm": gain(ks[18], (L, D_INNER)),
        "w_out": dense(ks[19], (L, MIX_WIDTH_2, D_MODEL), MIX_WIDTH_2),
        "ffn_pre_norm": gain(ks[20], (L, D_MODEL)),
        "ffn_post_norm": gain(ks[21], (L, D_MODEL)),
        "w_up": dense(ks[22], (L, D_MODEL, 2 * D_FF), D_MODEL),
        "ffn_conv_w": dense(ks[23], (L, FFN_CONV, D_FF), FFN_CONV),
        "ffn_conv_b": bias(ks[24], (L, D_FF)),
        "w_down": dense(ks[25], (L, D_FF, D_MODEL), D_FF),
    }

def second_block(x, c, ctx, c_ctx, w_mod, b_mod, mix_pre_norm, mix_post_norm, w_in, q_norm, w_q_up,
              kv_norm, w_kv_up, ssd_conv_w, ssd_conv_b, ssd_a_log, ssd_dt_bias, ssd_d, ssd_norm, w_out,
              ffn_pre_norm, ffn_post_norm, w_up, ffn_conv_w, ffn_conv_b, w_down):
    bsz, seq, _ = x.shape
    cos, sin = axial_rope_tables_2(seq)
    cos_q, sin_q = cos[:, None, :], sin[:, None, :]

    def flip(t):
        return jnp.flip(t, axis=1)

    for l in range(DEPTH_2):
        last = l == DEPTH_2 - 1
        mod_x = jnp.split((jax.nn.silu(c) @ w_mod[l] + b_mod[l])[:, None, :], N_MOD, axis=-1)
        mod_c = jnp.split((jax.nn.silu(c_ctx) @ w_mod[l] + b_mod[l])[None, None, :], N_MOD, axis=-1)

        cq_x, ckv_x, kr_x, z_x, xbc_x, dt_x = in_split(
            modulate(rms_norm_2(x, mix_pre_norm[l]), mod_x[0], mod_x[1]) @ w_in[l])
        cq_c, ckv_c, kr_c, z_c, xbc_c, dt_c = in_split(
            modulate(rms_norm_2(ctx, mix_pre_norm[l]), mod_c[0], mod_c[1]) @ w_in[l])

        q_nope_x, q_rope_x = mla_queries(cq_x, q_norm[l], w_q_up[l])
        q_rope_x = apply_rope_2(q_rope_x, cos_q, sin_q)
        k_nope_x, v_x = mla_keys_values(ckv_x, kv_norm[l], w_kv_up[l])
        k_rope_x = apply_rope_2(kr_x, cos, sin)
        k_nope_c, v_c = mla_keys_values(ckv_c, kv_norm[l], w_kv_up[l])
        attn_x = latent_attention(q_nope_x, q_rope_x,
                                  jnp.concatenate([k_nope_c, k_nope_x], axis=1),
                                  jnp.concatenate([kr_c, k_rope_x], axis=1),
                                  jnp.concatenate([v_c, v_x], axis=1))

        A = -jnp.exp(ssd_a_log[l].astype(jnp.float32)).reshape(2, SSD_GROUPS, HEADS_PER_GROUP)
        xs_x, b_x, c_x, dtv_x = ssd_prepare(xbc_x, dt_x, ssd_conv_w[l], ssd_conv_b[l], ssd_dt_bias[l])
        xs_c, b_c, c_c, dtv_c = ssd_prepare(xbc_c, dt_c, ssd_conv_w[l], ssd_conv_b[l], ssd_dt_bias[l])
        zero_state = jnp.zeros((bsz, SSD_GROUPS, HEADS_PER_GROUP, SSD_HEAD_DIM, SSD_STATE), xs_x.dtype)
        st_cf = ssd_states(xs_c, dtv_c[:, :, 0], A[0], b_c, c_c, zero_state)
        st_cb = ssd_states(flip(xs_c), flip(dtv_c[:, :, 1]), A[1], flip(b_c), flip(c_c), zero_state)
        st_xf = ssd_states(xs_x, dtv_x[:, :, 0], A[0], b_x, c_x, st_cf[2])
        st_xb = ssd_states(flip(xs_x), flip(dtv_x[:, :, 1]), A[1], flip(b_x), flip(c_x), st_cb[2])
        y_x = ssd_output(st_xf[0], st_xf[1]) + flip(ssd_output(st_xb[0], st_xb[1]))
        ssd_x = ssd_finish(y_x, xs_x, z_x, ssd_d[l], ssd_norm[l])

        mix_x = jnp.concatenate([attn_x, ssd_x], axis=-1) @ w_out[l]
        x = x + mod_x[2] * rms_norm_2(mix_x, mix_post_norm[l])

        if not last:
            q_nope_c, q_rope_c = mla_queries(cq_c, q_norm[l], w_q_up[l])
            attn_c = attend_2(q_nope_c, q_rope_c, k_nope_c, kr_c, v_c).reshape(bsz, -1, ATTN_WIDTH)
            y_c = ssd_output(st_cf[0], st_cf[1]) + flip(ssd_output(st_cb[0], st_cb[1]))
            ssd_c = ssd_finish(y_c, xs_c, z_c, ssd_d[l], ssd_norm[l])
            mix_c = jnp.concatenate([attn_c, ssd_c], axis=-1) @ w_out[l]
            ctx = ctx + mod_c[2] * rms_norm_2(mix_c, mix_post_norm[l])
            ffn_c = conv_glu(modulate(rms_norm_2(ctx, ffn_pre_norm[l]), mod_c[3], mod_c[4]),
                             w_up[l], ffn_conv_w[l], ffn_conv_b[l], w_down[l])
            ctx = ctx + mod_c[5] * rms_norm_2(ffn_c, ffn_post_norm[l])

        ffn_x = conv_glu(modulate(rms_norm_2(x, ffn_pre_norm[l]), mod_x[3], mod_x[4]),
                         w_up[l], ffn_conv_w[l], ffn_conv_b[l], w_down[l])
        x = x + mod_x[5] * rms_norm_2(ffn_x, ffn_post_norm[l])
    return x


def setup_inputs(seed=0):
    out = dict(first_inputs(seed))
    for name, value in second_inputs(seed + 1).items():
        if name != "x":
            out[name + "_2"] = value
    return out


def reference(
    x, c, ctx, c_ctx, norm_g, w_mod, b_mod, w_in, conv_w, q_norm_g, k_norm_g, hgrn_lb,
    hgrn_norm_g, w_out, final_g, c_2, ctx_2, c_ctx_2, w_mod_2, b_mod_2, mix_pre_norm_2,
    mix_post_norm_2, w_in_2, q_norm_2, w_q_up_2, kv_norm_2, w_kv_up_2, ssd_conv_w_2,
    ssd_conv_b_2, ssd_a_log_2, ssd_dt_bias_2, ssd_d_2, ssd_norm_2, w_out_2, ffn_pre_norm_2,
    ffn_post_norm_2, w_up_2, ffn_conv_w_2, ffn_conv_b_2, w_down_2,
):
    x = first_block(
        x, c, ctx, c_ctx, norm_g, w_mod, b_mod, w_in, conv_w, q_norm_g, k_norm_g, hgrn_lb,
        hgrn_norm_g, w_out, final_g,
    )
    return second_block(
        x, c_2, ctx_2, c_ctx_2, w_mod_2, b_mod_2, mix_pre_norm_2, mix_post_norm_2, w_in_2,
        q_norm_2, w_q_up_2, kv_norm_2, w_kv_up_2, ssd_conv_w_2, ssd_conv_b_2, ssd_a_log_2,
        ssd_dt_bias_2, ssd_d_2, ssd_norm_2, w_out_2, ffn_pre_norm_2, ffn_post_norm_2, w_up_2,
        ffn_conv_w_2, ffn_conv_b_2, w_down_2,
    )


_drawn_inputs = setup_inputs


def setup_inputs(seed=0):
    import zlib

    import numpy as np

    out = dict(_drawn_inputs(seed))
    spreads = {}
    factors = {'ctx': 8.0,
     'c_ctx': 6.066,
     'q_norm_g': 8.0,
     'k_norm_g': 8.0,
     'hgrn_lb': 5.538,
     'hgrn_norm_g': 3.657,
     'ctx_2': 3.024,
     'q_norm_2': 8.0,
     'ssd_conv_b_2': 5.704,
     'ssd_d_2': 7.409,
     'ffn_conv_b_2': 8.0}
    for name, (base, spread) in spreads.items():
        noise = np.random.default_rng([zlib.crc32(name.encode()), seed]).standard_normal(out[name].shape)
        drawn = base * np.exp(spread * noise) if base else spread * noise
        out[name] = __import__('jax').numpy.asarray(drawn.astype(out[name].dtype))
    for name, factor in factors.items():
        out[name] = (out[name] * factor).astype(out[name].dtype)
    return out
```

```python
import numpy as np
import concourse.bass as bass
import concourse.mybir as mybir
from contextlib import ExitStack
from concourse.alu_op_type import AluOpType as ALU

ACT = mybir.ActivationFunctionType
AX = mybir.AxisListType
F32 = mybir.dt.float32
U32 = mybir.dt.uint32

P = 128
D = 1024
KD = D // P
CTX, LAT = 256, 1024
T = CTX + LAT
NT, CT_, = T // P, CTX // P
BR = 256
EPS = 1e-6
HD = 64
HALF = 512

ALL_BLOCKS = [(0, CTX), (CTX, HALF), (CTX + HALF, HALF)]
LAT_BLOCKS = ALL_BLOCKS[1:]

O_CB, O_CC, O_CV, O_CZ, O_Q, O_AZ = 0, 256, 512, 768, 1024, 1536
O_HQ, O_FF, O_FB, O_HI, O_HZ, O_FU, O_FZ = 1792, 2048, 2304, 2560, 2816, 3072, 3328
QL, KVL, RD, NOPE = 384, 256, 32, 64
NH2 = 16
XBC = 1536
O2_CQ, O2_Z, O2_XBC, O2_DT = 0, QL + KVL + RD, QL + KVL + RD + D, QL + KVL + RD + D + XBC
DFF = 2816
KF = DFF // P
NMOD = 2 * 3 * D + 6 * D
M2 = 2 * 3 * D

A_W = 0
W_SLOTS, W_BYTES = 3, KD * HALF * 4
A_A = A_W + W_SLOTS * W_BYTES
A_B = A_A + NT * D * 4
A_R = A_B + NT * D * 4
A_C = A_R + 77 * 1024


class K:

    def __init__(self, nc, dram, out):
        self.nc, self.d, self.out = nc, dram, out
        self.base = None
        self.n = 0

    def at(self, name, shape, offset, dt=F32):
        self.n += 1
        return self.nc.alloc_sbuf_tensor_at(f"{name}_{self.n}", shape, dt, offset=self.base + offset)

    def sems(self, *names):
        self.n += 1
        return [self.nc.alloc_semaphore(f"{n}_{self.n}") for n in names]

    def done(self, sems):
        self.nc.clear_and_free_semaphores(list(sems))
        self.nc.all_engine_barrier(sem_only=True)


class Layout:

    def __init__(self, k, offset, end):
        self.k, self.o, self.end = k, offset, end

    def __call__(self, name, shape, dt=F32):
        size = int(np.prod(shape[1:])) * 4
        size = (size + 31) // 32 * 32
        assert self.o + size <= self.end, (name, self.o + size - self.end)
        t = self.k.at(name, shape, self.o, dt)
        self.o += size
        return t


class WeightStream:

    def __init__(self, k, chunks):
        self.k, self.chunks = k, chunks
        self.ring = [k.at(f"w{i}", [P, KD, HALF], A_W + i * W_BYTES) for i in range(W_SLOTS)]
        self.landed = [k.nc.alloc_semaphore(f"weights_landed{i}") for i in range(W_SLOTS)]
        self.products = k.nc.alloc_semaphore("products")
        self.count = 0
        self.end = {}
        self.loaded = 0
        self.taken = 0

    def take(self, n):
        first = self.taken
        self.taken += n
        assert self.taken <= len(self.chunks)
        return range(first, first + n)

    def tile(self, c):
        _, kt, cols = self.chunks[c]
        return self.ring[c % W_SLOTS][:, 0:kt, 0:cols]

    def load_until(self, sp, last):
        while self.loaded < min(last + W_SLOTS, len(self.chunks)):
            c = self.loaded
            if c >= W_SLOTS and c - W_SLOTS not in self.end:
                break
            if c >= W_SLOTS:
                sp.wait_ge(self.products, self.end[c - W_SLOTS])
            sp.dma_start(self.tile(c), self.chunks[c][0].rearrange("(k p) n -> p k n", p=P)).then_inc(
                self.landed[c % W_SLOTS], 16)
            self.loaded += 1

    def wait(self, pe, c):
        pe.wait_ge(self.landed[c % W_SLOTS], 16 * (c // W_SLOTS + 1))


def weight_plan(d):
    plan = []

    def cols(w, a, b, step=HALF):
        for c in range(a, b, step):
            n = min(step, b - c)
            rows = w.shape[0]
            for r in range(0, rows, D):
                m = min(D, rows - r)
                plan.append((w[r:r + m, c:c + n], m // P, n))

    for layer in range(2):
        cols(d["w_mod"][layer], 0, 3 * D)
    cols(d["w_mod_2"][0], 0, 6 * D)
    for layer in range(2):
        w = d["w_in"][layer]
        cols(w, O_CB, O_Q)
        cols(w, O_Q, O_AZ)
        cols(w, O_AZ, O_HQ, 256)
        cols(w, O_HQ, O_FF, 256)
        cols(w, O_HI, O_HZ, 256)
        cols(w, O_HZ, O_FU, 256)
        cols(w, O_FF, O_FB, 256)
        cols(w, O_FB, O_HI, 256)
        cols(w, O_FU, O_FZ, 256)
        cols(w, O_FZ, 3584, 256)
        if layer == 0:
            cols(d["dft_ctx"], 0, CTX)
        cols(d["dft_lat"], 0, LAT)
        cols(d["w_out"][layer], 0, D)
    w = d["w_in_2"][0]
    cols(w, 0, 512)
    cols(w, 512, O2_Z)
    cols(w, O2_Z, O2_XBC)
    cols(w, O2_XBC, O2_DT)
    cols(w, O2_DT, O2_DT + 32)
    cols(d["w_out_2"][0], 0, D)
    for j in range(0, DFF, 256):
        cols(d["w_up_2"][0], j, j + 256)
        cols(d["w_up_2"][0], DFF + j, DFF + j + 256)
    cols(d["w_down_2"][0], 0, D)
    return plan


def project(k, jobs):
    nc, ws, ps = k.nc, k.ws, k.ps
    evac_act, evac_dve = sems = k.sems("evacuated_by_act", "evacuated_by_dve")
    done_of = {"act": evac_act, "dve": evac_dve}
    groups, plan = [], []
    load = {"act": 0, "dve": 0}
    count = {"act": 0, "dve": 0}
    for j in jobs:
        chunks = ws.take((j["kt"] + KD - 1) // KD)
        subs = range((j["cols"] + P - 1) // P) if j["mode"] == "fm" else [0]
        mine = []
        for s in subs:
            for n, (t0, tn) in enumerate(j["toks"]):
                m = min(P, j["cols"] - s * P) if j["mode"] == "fm" else tn
                free = tn if j["mode"] == "fm" else j["cols"]
                do = "silu" if s >= j.get("silu_from", 99) else j["do"]
                by = {"mul": "dve", "silu": "act"}.get(do)
                by = by or ("act" if load["act"] <= load["dve"] else "dve")
                load[by] += free + 150
                count[by] += 1
                g = dict(job=j, do=do, sub=s, n=n, t0=t0, tn=tn, by=by, count=count[by],
                         out=ps[0:m, len(groups) % 8, 0:free],
                         before=groups[len(groups) - 8] if len(groups) >= 8 else None)
                groups.append(g)
                mine.append(g)
        assert len(chunks) == 1 or len(mine) <= 8
        for c in chunks:
            assert ws.chunks[c][2] == j["cols"], (c, ws.chunks[c][1:], j["cols"])
            for g in mine:
                ws.count += 1
                g["ready"] = ws.count
            ws.end[c] = ws.count
        plan.append((j, chunks, mine))

    with nc.Block() as block:
        @block.sync
        def _(sp):
            ws.load_until(sp, ws.taken)

        @block.tensor
        def _(pe):
            for j, chunks, mine in plan:
                for ci, c in enumerate(chunks):
                    ws.wait(pe, c)
                    w, kt = ws.tile(c), ws.chunks[c][1]
                    for g in mine:
                        if ci == 0 and g["before"]:
                            pe.wait_ge(done_of[g["before"]["by"]], g["before"]["count"])
                        for kk in range(kt):
                            kx = ci * KD + kk
                            x = j["x"](kx, g["t0"], g["tn"])
                            if j["mode"] == "fm":
                                c0 = g["sub"] * P
                                lhs, rhs = w[:, kk, c0:c0 + g["out"].shape[0]], x
                            else:
                                lhs, rhs = x, w[:, kk, :]
                            mm = pe.matmul(g["out"], lhs, rhs, start=(kx == 0), stop=(kx == j["kt"] - 1))
                        mm.then_inc(ws.products, 1)

        @block.scalar
        def _(act):
            for g in groups:
                if g["by"] == "act":
                    dst = g["job"]["dst"](g["sub"], g["n"])
                    act.wait_ge(ws.products, g["ready"])
                    func = ACT.Silu if g["do"] == "silu" else ACT.Copy
                    act.activation(dst, g["out"], func).then_inc(evac_act, 1)

        @block.vector
        def _(dve):
            for g in groups:
                if g["by"] == "dve":
                    dst = g["job"]["dst"](g["sub"], g["n"])
                    dve.wait_ge(ws.products, g["ready"])
                    if g["do"] == "mul":
                        dve.tensor_tensor(dst, g["out"], dst, ALU.mult).then_inc(evac_dve, 1)
                    else:
                        dve.tensor_copy(dst, g["out"]).then_inc(evac_dve, 1)

    k.done(sems)


def modulation(k):
    nc, ws, ps, d = k.nc, k.ws, k.ps, k.d
    lay = Layout(k, A_A, A_R)
    cond = lay("cond", [P, 4, KD])
    act_c = lay("act_c", [P, 4, KD])
    bias = [lay(f"bias{i}", [2, HALF]) for i in range(4)]
    res = [lay(f"res{i}", [2, HALF]) for i in range(4)]
    n = NMOD // HALF
    chunks = ws.take(n)
    base = ws.count
    for i, c in enumerate(chunks):
        ws.end[c] = base + i + 1
    ws.count += n
    cond_in, silu_done, summed = sems = k.sems("cond_in", "silu_done", "summed")
    bias_in = k.sems(*[f"bias_in{i}" for i in range(4)])
    stored = k.sems(*[f"mod_stored{i}" for i in range(4)])
    bsrc = [d["b_mod"][0:1, :], d["b_mod"][1:2, :], d["b_mod_2"][0:1, :]]

    def bias_of(i):
        row = i * HALF
        which = 0 if row < 3 * D else 1 if row < M2 else 2
        off = row - (0, 3 * D, M2)[which]
        return bsrc[which][:, off:off + HALF].to_broadcast([2, HALF])

    with nc.Block() as block:
        @block.sync
        def _(sp):
            for i, name in enumerate(("c", "c_ctx", "c_2", "c_ctx_2")):
                src = d[name] if len(d[name].shape) == 1 else d[name][0]
                sp.dma_start(cond[:, i, :], src.rearrange("(k p) -> p k", p=P)).then_inc(cond_in, 16)
            ws.load_until(sp, ws.taken)

        @block.gpsimd
        def _(pool):
            for i in range(n):
                if i >= 4:
                    pool.wait_ge(summed, i - 3)
                pool.dma_start(bias[i % 4][:, :], bias_of(i)).then_inc(bias_in[i % 4], 16)

        @block.scalar
        def _(act):
            act.wait_ge(cond_in, 64)
            act.activation(act_c[:, :, :], cond[:, :, :], ACT.Silu).then_inc(silu_done, 1)
            for i in range(n):
                act.wait_ge(summed, i + 1)
                act.dma_start(d["mod"][:, i * HALF:(i + 1) * HALF], res[i % 4][:, :]).then_inc(stored[i % 4], 16)
            for i in range(4):
                act.wait_ge(stored[i], 16 * ((n - i + 3) // 4))

        @block.tensor
        def _(pe):
            pe.wait_ge(silu_done, 1)
            for i, c in enumerate(chunks):
                ws.wait(pe, c)
                if i >= 8:
                    pe.wait_ge(summed, i - 7)
                s = 0 if i * HALF < M2 else 2
                for kk in range(KD):
                    mm = pe.matmul(ps[0:2, i % 8, :], act_c[:, s:s + 2, kk], ws.tile(c)[:, kk, :],
                                   start=(kk == 0), stop=(kk == KD - 1))
                mm.then_inc(ws.products, 1)

        @block.vector
        def _(dve):
            for i in range(n):
                dve.wait_ge(ws.products, base + i + 1)
                dve.wait_ge(bias_in[i % 4], 16 * (i // 4 + 1))
                if i >= 4:
                    dve.wait_ge(stored[i % 4], 16 * (i // 4))
                dve.tensor_tensor(res[i % 4][:, :], ps[0:2, i % 8, :], bias[i % 4][:, :],
                                  ALU.add).then_inc(summed, 1)
    k.done(sems + bias_in + stored)


def normalize(k, tiles, xt, mod_cols, gain, lay, y=None, gates=None, post=None, pre=None,
              stored=None):
    nc, ps, d = k.nc, k.ps, k.d
    NX = 3
    xs = [lay(f"x{i}", [P, D]) for i in range(NX)]
    tmp = [lay(f"tmp{i}", [P, D]) for i in range(2)]
    xn = [lay(f"xn{i}", [P, D]) for i in range(2)]
    nt = len(tiles)
    stat = lay("stat", [P, 3, 3, nt])
    streams = sorted({w["stream"] for w in tiles})
    gate_row = {s: lay(f"gate_row{s}", [P, D]) for s in sorted({w["stream"] for w in tiles if w["res"]})
                } if gates is not None else {}
    post_row = lay("post_row", [P, D]) if post is not None else None
    pre_row = lay("pre_row", [P, D]) if pre is not None else None
    cols = lay("mod_cols", [P, 2, 2, KD])
    gcol = lay("gain_col", [P, KD])
    sems = k.sems("rows_in", "cols_in", "squared", "rooted", "dve_chain", "scaled",
                  "transposed", "evac_act", "evac_dve", "gate_ready")
    (rows_in, cols_in, squared, rooted, chain, scaled, transposed, evac_act, evac_dve, gate_ready) = sems
    x_in = k.sems(*[f"x_in{i}" for i in range(NX)])
    sems = sems + x_in
    if stored is None:
        stored = k.sems(*[f"sum_stored{i}" for i in range(NX)])
        sems = sems + stored
    n_rows = len(gate_row) + (post is not None) + (pre is not None)
    n_cols = (2 * len(streams) if mod_cols else 0) + 1
    n_store = [0] * NX

    def norms_of(w):
        return ((["post"] if post is not None and w["res"] else []) + (["pre"] if pre is not None and w["res"] else [])
                + (["main"] if xt is not None else []))

    sq_index, i = {}, 0
    for n, w in enumerate(tiles):
        for kind in norms_of(w):
            i += 1
            sq_index[n, kind] = i
    slot_of = {"post": 0, "pre": 1, "main": 2}
    chained = [0]
    step_ready = {}
    store_ready = {}

    with nc.Block() as block:
        @block.gpsimd
        def _(pool):
            if xt is not None:
                for s in streams if mod_cols else ():
                    for j in range(2):
                        o = mod_cols[j]
                        pool.dma_start(cols[:, s, j, :], d["mod"][s, o:o + D].rearrange("(k p) -> p k", p=P)
                                       ).then_inc(cols_in, 16)
                pool.dma_start(gcol[:, :], gain.rearrange("(k p) -> p k", p=P)).then_inc(cols_in, 16)

        @block.vector
        def _(dve):
            def link(ins):
                ins.then_inc(chain, 1)
                chained[0] += 1
                dve.wait_ge(chain, chained[0])
                return chained[0]

            if xt is not None:
                dve.wait_ge(cols_in, 16 * n_cols)
                if not mod_cols:
                    link(dve.memset(cols[:, 0, 0, :], 0.0))
                    link(dve.tensor_copy(cols[:, 0, 1, :], gcol[:, :]))
                for s in streams if mod_cols else ():
                    link(dve.scalar_tensor_tensor(cols[:, s, 1, :], cols[:, s, 1, :], 1.0, gcol[:, :],
                                                  ALU.add, ALU.mult))
            if n_rows:
                dve.wait_ge(rows_in, 16 * n_rows)
            if post is not None:
                for s in gate_row:
                    link(dve.tensor_tensor(gate_row[s][:, :], gate_row[s][:, :], post_row[:, :], ALU.mult))
            dve.sem_inc(gate_ready, 1)

            def mean_root(n, kind):
                dve.wait_ge(squared, sq_index[n, kind])
                st = stat[:, slot_of[kind], :, n]
                dve.tensor_scalar(st[:, 1:2], st[:, 0:1], 1.0 / D, EPS, ALU.mult, ALU.add).then_inc(chain, 1)
                chained[0] += 1
                step_ready[n, kind] = chained[0]
                dve.wait_ge(rooted, sq_index[n, kind])
                link(dve.reciprocal(st[:, 2:3], st[:, 1:2]))
                return st[:, 2:3]

            def transposes_out(n):
                w = tiles[n]
                dve.wait_ge(transposed, 2 * n + 2)
                for q in range(4):
                    kk = 4 + q
                    ins = dve.tensor_scalar(xt[:, kk, w["t"] * P:(w["t"] + 1) * P],
                                            ps[:, 4 + 2 * (n % 2) + 1, q * P:(q + 1) * P],
                                            cols[:, w["stream"], 1, kk:kk + 1], cols[:, w["stream"], 0, kk:kk + 1],
                                            ALU.mult, ALU.add)
                ins.then_inc(evac_dve, 1)

            for n, w in enumerate(tiles):
                x = xs[n % NX]
                if w["res"]:
                    yt = y[:, w["yt"], :]
                    g = gate_row.get(w["stream"])
                    if gates is None:
                        pass
                    elif post is not None:
                        r = mean_root(n, "post")
                        link(dve.scalar_tensor_tensor(tmp[n % 2][:, :], yt, r, g[:, :], ALU.mult, ALU.mult))
                    else:
                        link(dve.tensor_tensor(tmp[n % 2][:, :], yt, g[:, :], ALU.mult))
                    dve.wait_ge(x_in[n % NX], 16 * (n // NX + 1))
                    if gates is None:
                        step_ready[n, "sum"] = link(dve.tensor_tensor(x[:, :], yt, x[:, :], ALU.mult))
                    else:
                        step_ready[n, "sum"] = link(dve.tensor_tensor(x[:, :], tmp[n % 2][:, :], x[:, :], ALU.add))
                    if pre is not None:
                        r = mean_root(n, "pre")
                        step_ready[n, "sum2"] = link(dve.scalar_tensor_tensor(
                            x[:, :], x[:, :], r, pre_row[:, :], ALU.mult, ALU.mult))
                else:
                    dve.wait_ge(x_in[n % NX], 16 * (n // NX + 1))
                store_ready[n] = chained[0]
                if xt is not None:
                    if n >= 2:
                        dve.wait_ge(transposed, 2 * (n - 2) + 2)
                    r = mean_root(n, "main")
                    dve.tensor_scalar(xn[n % 2][:, :], x[:, :], r, None, ALU.mult).then_inc(scaled, 1)
                    if n >= 1:
                        transposes_out(n - 1)
            if xt is not None:
                transposes_out(nt - 1)

        @block.scalar
        def _(act):
            def square_root(n, kind, data):
                st = stat[:, slot_of[kind], :, n]
                act.activation(ps[:, 0:2, :].rearrange("p a b -> p (a b)"), data, ACT.Square,
                               accum_out=st[:, 0:1]).then_inc(squared, 1)
                act.wait_ge(chain, step_ready[n, kind])
                act.activation(st[:, 1:2], st[:, 1:2], ACT.Sqrt).then_inc(rooted, 1)

            def transposes_out(n):
                w = tiles[n]
                act.wait_ge(transposed, 2 * n + 1)
                act.wait_ge(gate_ready, 1)
                for kk in range(4):
                    ins = act.activation(xt[:, kk, w["t"] * P:(w["t"] + 1) * P],
                                         ps[:, 4 + 2 * (n % 2), kk * P:(kk + 1) * P], ACT.Identity,
                                         bias=cols[:, w["stream"], 0, kk:kk + 1],
                                         scale=cols[:, w["stream"], 1, kk:kk + 1])
                ins.then_inc(evac_act, 1)

            for n, w in enumerate(tiles):
                x = xs[n % NX]
                if w["res"]:
                    if post is not None:
                        square_root(n, "post", y[:, w["yt"], :])
                    if pre is not None:
                        act.wait_ge(chain, step_ready[n, "sum"])
                        square_root(n, "pre", x[:, :])
                if xt is not None:
                    if w["res"]:
                        act.wait_ge(chain, step_ready[n, "sum2" if pre is not None else "sum"])
                    else:
                        act.wait_ge(x_in[n % NX], 16 * (n // NX + 1))
                    square_root(n, "main", x[:, :])
                    if n >= 1:
                        transposes_out(n - 1)
            if xt is not None:
                transposes_out(nt - 1)

        @block.tensor
        def _(pe):
            if xt is not None:
                for n, w in enumerate(tiles):
                    pe.wait_ge(scaled, n + 1)
                    for half in range(2):
                        if n >= 2:
                            pe.wait_ge((evac_act, evac_dve)[half], n - 1)
                        for q in range(4):
                            kk = 4 * half + q
                            mm = pe.transpose(ps[:, 4 + 2 * (n % 2) + half, q * P:(q + 1) * P],
                                              xn[n % 2][:, kk * P:(kk + 1) * P], k.ident[:, :])
                        mm.then_inc(transposed, 1)

        @block.sync
        def _(sp):
            for s in gate_row:
                sp.dma_start(gate_row[s][:, :], d["mod"][s:s + 1, gates:gates + D].to_broadcast([P, D])
                             ).then_inc(rows_in, 16)
            if post is not None:
                sp.dma_start(post_row[:, :], post.unsqueeze(0).to_broadcast([P, D])).then_inc(rows_in, 16)
            if pre is not None:
                sp.dma_start(pre_row[:, :], pre.unsqueeze(0).to_broadcast([P, D])).then_inc(rows_in, 16)

            def store(n):
                w = tiles[n]
                if w["store"] is not None:
                    if w["res"]:
                        sp.wait_ge(chain, store_ready[n])
                    sp.dma_start(w["store"], xs[n % NX][:, :]).then_inc(stored[n % NX], 16)
                    n_store[n % NX] += 1

            for n, w in enumerate(tiles):
                if n >= NX:
                    if xt is not None:
                        sp.wait_ge(scaled, n - NX + 1)
                    if n_store[n % NX]:
                        sp.wait_ge(stored[n % NX], 16 * n_store[n % NX])
                sp.dma_start(xs[n % NX][:, :], w["src"]).then_inc(x_in[n % NX], 16)
                if n >= 1:
                    store(n - 1)
            store(nt - 1)
            for i in range(NX):
                if n_store[i]:
                    sp.wait_ge(stored[i], 16 * n_store[i])
            if k.ws.loaded:
                k.ws.load_until(sp, k.ws.taken)
    k.done(sems)


def conv_branch(k, layer, parts, yt):
    nc, d = k.nc, k.d
    cb, cc, cv, cz = parts
    lay = Layout(k, A_C - 1024, A_C)
    taps = lay("taps", [P, 2, 3])
    taps_in, chain = sems = k.sems("taps_in", "dve_chain")
    with nc.Block() as block:
        @block.sync
        def _(sp):
            for j in range(3):
                sp.dma_start(taps[:, :, j], d["conv_w"][layer, j].rearrange("(c p) -> p c", p=P)).then_inc(taps_in, 16)
            k.ws.load_until(sp, k.ws.taken)

        @block.vector
        def _(dve):
            n = [0]

            def link(ins):
                ins.then_inc(chain, 1)
                n[0] += 1
                dve.wait_ge(chain, n[0])

            dve.wait_ge(taps_in, 48)
            link(dve.tensor_tensor(cc[:, :, :], cc[:, :, :], cv[:, :, :], ALU.mult))
            for c in range(2):
                u, t = cc[:, c, :], cv[:, c, :]
                link(dve.tensor_scalar(t, u, taps[:, c, 1:2], None, ALU.mult))
                for s0, sn in ((0, CTX), (CTX, LAT)):
                    a, b = s0, s0 + sn
                    link(dve.scalar_tensor_tensor(t[:, a + 1:b], u[:, a:b - 1], taps[:, c, 0:1], t[:, a + 1:b],
                                                  ALU.mult, ALU.add))
                    link(dve.scalar_tensor_tensor(t[:, a:b - 1], u[:, a + 1:b], taps[:, c, 2:3], t[:, a:b - 1],
                                                  ALU.mult, ALU.add))
            link(dve.tensor_tensor(cb[:, :, :], cb[:, :, :], cz[:, :, :], ALU.mult))
            link(dve.tensor_tensor(yt[:, 0:2, :], cb[:, :, :], cv[:, :, :], ALU.mult))
    k.done(sems)


def heads_prepare(k, layer, qkv, qt, kt, v, lay):
    nc, d, ps = k.nc, k.d, k.ps
    NH, NQ = 6, 4
    gains = lay("gains", [P, NH, HD])
    cos = lay("cos", [P, LAT // P, HD // 2])
    sin = lay("sin", [P, LAT // P, HD // 2])
    sq = [lay(f"sq{i}", [P, NH, HD]) for i in range(2)]
    t1 = lay("t1", [P, NH, HD // 2])
    t2 = lay("t2", [P, NH, HD // 2])
    stat = lay("stat", [P, NT, NH])
    (tables_in, chain, mean_done, rooted, turned, transposed, q_out, k_out, ones_done) = sems = k.sems(
        "tables_in", "dve_chain", "mean_done", "rooted", "turned", "transposed", "q_out", "k_out", "ones_done")
    with nc.Block() as block:
        @block.sync
        def _(sp):
            for h in range(NH):
                g = d["q_norm_g"] if h < NQ else d["k_norm_g"]
                sp.dma_start(gains[:, h, :], g[layer:layer + 1, :].to_broadcast([P, HD])).then_inc(tables_in, 16)
            sp.dma_start(cos[:, :, :], d["rope1"][0].rearrange("(t p) f -> p t f", p=P)).then_inc(tables_in, 16)
            sp.dma_start(sin[:, :, :], d["rope1"][1].rearrange("(t p) f -> p t f", p=P)).then_inc(tables_in, 16)
            k.ws.load_until(sp, k.ws.taken)

        @block.gpsimd
        def _(pool):
            for g in range(2):
                src = qkv[:, :, NH * HD + g * HD:NH * HD + (g + 1) * HD]
                pool.memset(v[:, :, g, HD:2 * HD], 1.0)
                pool.tensor_copy(v[:, :, g, 0:HD], src)
                pool.tensor_copy(v[:, :, g, 2 * HD:3 * HD], src)
        @block.vector
        def _(dve):
            n = [0]

            def link(ins):
                ins.then_inc(chain, 1)
                n[0] += 1
                dve.wait_ge(chain, n[0])

            dve.memset(kt[HD:HD + 1, :, :], 1.0)
            for t in range(NT):
                x = qkv[:, t, 0:NH * HD].rearrange("p (h e) -> p h e", h=NH)
                link(dve.tensor_tensor(sq[t % 2][:, :, :], x, x, ALU.mult))
                link(dve.tensor_reduce(stat[:, t, :], sq[t % 2][:, :, :], AX.X, ALU.add))
            dve.tensor_scalar(stat[:, :, :], stat[:, :, :], 1.0 / HD, EPS, ALU.mult, ALU.add).then_inc(mean_done, 1)
            dve.wait_ge(rooted, 1)
            link(dve.reciprocal(stat[:, :, :], stat[:, :, :]))
            dve.wait_ge(tables_in, 16 * (NH + 2))

            def k_evacuate(t):
                dve.wait_ge(transposed, t + 1)
                dve.tensor_copy(kt[0:HD, :, t * P:(t + 1) * P],
                                ps[0:HD, 4 + t % 2, 0:2 * P].rearrange("p (h c) -> p h c", h=2)).then_inc(k_out, 1)

            for t in range(NT):
                x = qkv[:, t, 0:NH * HD].rearrange("p (h e) -> p h e", h=NH)
                link(dve.tensor_tensor(x, x, stat[:, t, :].unsqueeze(2).to_broadcast([P, NH, HD]), ALU.mult))
                last = dve.tensor_tensor(x, x, gains[:, :, :], ALU.mult)
                if t >= CT_:
                    link(last)
                    c = cos[:, t - CT_, :].unsqueeze(1).to_broadcast([P, NH, HD // 2])
                    s = sin[:, t - CT_, :].unsqueeze(1).to_broadcast([P, NH, HD // 2])
                    x1, x2 = x[:, :, 0:HD:2], x[:, :, 1:HD:2]
                    o1, o2 = sq[t % 2][:, :, 0:HD // 2], sq[t % 2][:, :, HD // 2:HD]
                    link(dve.tensor_tensor(o1, x1, c, ALU.mult))
                    link(dve.tensor_tensor(t1[:, :, :], x2, s, ALU.mult))
                    link(dve.tensor_tensor(o2, x1, s, ALU.mult))
                    link(dve.tensor_tensor(t2[:, :, :], x2, c, ALU.mult))
                    link(dve.tensor_tensor(x1, o1, t1[:, :, :], ALU.subtract))
                    last = dve.tensor_tensor(x2, o2, t2[:, :, :], ALU.add)
                last.then_inc(turned, 1)
                if t >= 1:
                    k_evacuate(t - 1)
            k_evacuate(NT - 1)

        @block.scalar
        def _(act):
            act.wait_ge(mean_done, 1)
            act.activation(stat[:, :, :], stat[:, :, :], ACT.Sqrt).then_inc(rooted, 1)
            for t in range(NT):
                act.wait_ge(transposed, t + 1)
                act.copy(qt[0:HD, :, t * P:(t + 1) * P],
                         ps[0:HD, t % 2, :].rearrange("p (h c) -> p h c", h=NQ)).then_inc(q_out, 1)

        @block.tensor
        def _(pe):
            for t in range(NT):
                pe.wait_ge(turned, t + 1)
                if t >= 2:
                    pe.wait_ge(q_out, t - 1)
                    pe.wait_ge(k_out, t - 1)
                for h in range(NH):
                    o = ps[0:HD, t % 2, h * P:(h + 1) * P] if h < NQ else ps[0:HD, 4 + t % 2, (h - NQ) * P:(h - NQ + 1) * P]
                    mm = pe.transpose(o, qkv[:, t, h * HD:(h + 1) * HD], k.ident[:, :])
                mm.then_inc(transposed, 1)
    k.done(sems)


def attention(k, units, lay, scale, gated):
    nc, ps = k.nc, k.ps
    NPT = 3
    pt = [lay(f"pt{i}", [P, HALF]) for i in range(NPT)]
    mx = [lay(f"mx{i}", [P, 4]) for i in range(2)]
    rec = lay("rec", [P, HALF])
    (s_ready, maxed, turned, row_set, st_ready, exped, pv_done, chain, normed) = sems = k.sems(
        "row_scores", "row_maxed", "max_turned", "max_row_set", "scores", "probs", "pv", "dve_chain", "normed")
    U = len(units)
    q0, k0 = [0], [0]
    for u in units:
        q0.append(q0[-1] + u["nq"] // P)
        k0.append(k0[-1] + u["nk"] // P)

    with nc.Block() as block:
        @block.sync
        def _(sp):
            k.ws.load_until(sp, k.ws.taken)

        @block.tensor
        def _(pe):
            def row_scores(u, i):
                w = units[u]
                r0, r1 = w["rows"]
                g = q0[u] + i
                if g >= 1:
                    pe.wait_ge(maxed, g)
                for b in range(0, w["nk"], HALF):
                    n = min(HALF, w["nk"] - b)
                    mm = pe.matmul(ps[:, b // HALF, 0:n], w["q"][r0:r1, i * P:(i + 1) * P],
                                   w["k"][r0:r1, b:b + n], start=True, stop=True)
                mm.then_inc(s_ready, 1)

            def turn(u):
                w = units[u]
                r = w["row"]
                pe.wait_ge(maxed, q0[u + 1])
                if u >= 1:
                    pe.wait_ge(row_set, u)
                for i in range(w["nq"] // P):
                    mm = pe.matmul(ps[r:r + 1, 3, i * P:(i + 1) * P], mx[u % 2][:, i:i + 1], k.ident[:, :],
                                   start=True, stop=True)
                mm.then_inc(turned, 1)

            def scores(u, i):
                w = units[u]
                r0, r1 = w["rows_max"]
                g = k0[u] + i
                if i == 0:
                    pe.wait_ge(row_set, u + 1)
                if g >= 2:
                    pe.wait_ge(exped, g - 1)
                pe.matmul(ps[:, 4 + g % 2, 0:w["nq"]], w["k"][r0:r1, i * P:(i + 1) * P], w["q"][r0:r1, :],
                          start=True, stop=True).then_inc(st_ready, 1)

            def pv(u, i):
                w = units[u]
                g, n = k0[u] + i, w["nk"] // P
                if i == 0 and u >= 2:
                    pe.wait_ge(normed, u - 1)
                pe.wait_ge(exped, g + 1)
                pe.matmul(ps[:, 6 + u % 2, 0:w["nq"]], w["v"](i), pt[g % NPT][:, 0:w["nq"]],
                          start=(i == 0), stop=(i == n - 1)).then_inc(pv_done, 1)

            for i in range(units[0]["nq"] // P):
                row_scores(0, i)
            turn(0)
            for u, w in enumerate(units):
                n = w["nk"] // P
                ahead = list(range(units[u + 1]["nq"] // P)) if u + 1 < U else []
                for i in range(n):
                    scores(u, i)
                    if i >= 1:
                        pv(u, i - 1)
                    if ahead and i % 2 == 1:
                        row_scores(u + 1, ahead.pop(0))
                pv(u, n - 1)
                for i in ahead:
                    row_scores(u + 1, i)
                if u + 1 < U:
                    turn(u + 1)

        @block.scalar
        def _(act):
            def row(u):
                w = units[u]
                r = w["row"]
                act.wait_ge(turned, u + 1)
                act.mul(w["q"][r:r + 1, :], ps[r:r + 1, 3, 0:w["nq"]], -1.0).then_inc(row_set, 1)

            row(0)
            for u, w in enumerate(units):
                for i in range(w["nk"] // P):
                    g = k0[u] + i
                    act.wait_ge(st_ready, g + 1)
                    if g >= NPT:
                        act.wait_ge(pv_done, g - NPT + 1)
                    act.activation(pt[g % NPT][:, 0:w["nq"]], ps[:, 4 + g % 2, 0:w["nq"]], ACT.Exp,
                                   scale=scale).then_inc(exped, 1)
                if u + 1 < U:
                    row(u + 1)

        @block.vector
        def _(dve):
            n = [0]

            def link(ins):
                ins.then_inc(chain, 1)
                n[0] += 1
                dve.wait_ge(chain, n[0])

            def maxima(u, i):
                w = units[u]
                dve.wait_ge(s_ready, q0[u] + i + 1)
                if i == 0 and u >= 2:
                    dve.wait_ge(turned, u - 1)
                nb = (w["nk"] + HALF - 1) // HALF
                src = ps[:, 0:nb, :].rearrange("p a b -> p (a b)")[:, 0:w["nk"]]
                dve.tensor_reduce(mx[u % 2][:, i:i + 1], src, AX.X, ALU.max).then_inc(maxed, 1)

            def normalise(u):
                w = units[u]
                a, b = (64, 0) if w["odd"] else (0, 64)
                nq, bank = w["nq"], 6 + u % 2
                dve.wait_ge(pv_done, k0[u + 1])
                link(dve.reciprocal(rec[a:a + 64, 0:nq], ps[b:b + 64, bank, 0:nq]))
                if gated:
                    link(dve.tensor_tensor(rec[a:a + 64, 0:nq], rec[a:a + 64, 0:nq], w["out"], ALU.mult))
                dve.tensor_tensor(w["out"], ps[a:a + 64, bank, 0:nq], rec[a:a + 64, 0:nq],
                                  ALU.mult).then_inc(normed, 1)
                dve.wait_ge(normed, u + 1)

            for u, w in enumerate(units):
                for i in range(w["nq"] // P):
                    maxima(u, i)
                if u >= 1:
                    normalise(u - 1)
            normalise(U - 1)
    k.done(sems)


LEVELS = [64, 32, 16, 8, 4, 2, 1]
NL = len(LEVELS)


def recurrence_gates(k, layer, direction, fx, key, lay):
    nc, d = k.nc, k.d
    e = [lay(f"e{i}", [P, T]) for i in range(2)]
    m = [lay(f"m{i}", [P, T]) for i in range(2)]
    ones = lay("ones", [P, 1])
    lbp = lay("lbp", [P, 2, 2])
    g = lay("g", [P, 8, 2])
    lb_in, chain, done = sems = k.sems("lb_in", "dve_chain", "act_done")
    LB = layer > 0
    ready = {}

    with nc.Block() as block:
        @block.sync
        def _(sp):
            if LB:
                for j in range(2):
                    sp.dma_start(lbp[:, j, :], d["hgrn_lb"][direction, j].rearrange("(c p) -> p c", p=P)
                                 ).then_inc(lb_in, 16)
            k.ws.load_until(sp, k.ws.taken)

        @block.vector
        def _(dve):
            n = [0]

            def link(ins):
                ins.then_inc(chain, 1)
                n[0] += 1
                dve.wait_ge(chain, n[0])
                return n[0]

            link(dve.memset(ones[:, :], 1.0))
            acts = 0
            if LB:
                dve.wait_ge(lb_in, 32)
                link(dve.tensor_tensor(g[:, 0, :], lbp[:, 1, :], lbp[:, 0, :], ALU.subtract))
                ready["g"] = link(dve.scalar_tensor_tensor(g[:, 1, :], g[:, 0, :], -1.0, g[:, 0, :], ALU.mult, ALU.max))
                link(dve.tensor_scalar(g[:, 6, :], g[:, 0, :], 0.0, None, ALU.min))
                link(dve.tensor_scalar(g[:, 7, :], g[:, 0, :], -1.0, 0.0, ALU.mult, ALU.min))
                acts = 3
                dve.wait_ge(done, acts)
                link(dve.tensor_tensor(g[:, 3, :], g[:, 6, :], g[:, 2, :], ALU.subtract))
                link(dve.tensor_tensor(g[:, 4, :], g[:, 7, :], g[:, 2, :], ALU.subtract))
            for c in range(2):
                ready["abs", c] = link(dve.scalar_tensor_tensor(e[c][:, :], fx[:, c, :], -1.0, fx[:, c, :], ALU.mult, ALU.max))
                ready["min", c] = link(dve.tensor_scalar(m[c][:, :], fx[:, c, :], 0.0, None, ALU.min))
            for c in range(2):
                acts += 3
                dve.wait_ge(done, acts)
                link(dve.tensor_tensor(m[c][:, :], m[c][:, :], e[c][:, :], ALU.subtract))
                if LB:
                    link(dve.tensor_scalar(m[c][:, :], m[c][:, :], g[:, 4, c:c + 1], None, ALU.add))
                    link(dve.tensor_scalar(e[c][:, :], m[c][:, :], g[:, 3, c:c + 1], None, ALU.subtract))
                    ready["abs2", c] = link(dve.scalar_tensor_tensor(e[c][:, :], e[c][:, :], -1.0, e[c][:, :], ALU.mult, ALU.max))
                    link(dve.tensor_scalar(m[c][:, :], m[c][:, :], g[:, 3, c:c + 1], None, ALU.max))
                    link(dve.tensor_scalar(key[:, c, :], key[:, c, :], g[:, 5, c:c + 1], None, ALU.mult))
                    acts += 2
                    dve.wait_ge(done, acts)
                    link(dve.tensor_tensor(m[c][:, :], m[c][:, :], e[c][:, :], ALU.add))
            for c in range(2):
                for t in range(NT):
                    a, b = t * P, (t + 1) * P
                    o, i = fx[:, c, a:b], m[c][:, a:b]
                    if direction:
                        o, i = fx[:, c, a:b][:, ::-1], m[c][:, a:b][:, ::-1]
                    dve.tensor_tensor_scan(o, ones[:, 0:1].to_broadcast([P, P]), i, 0.0, ALU.mult, ALU.add)

        @block.scalar
        def _(act):
            i = [0]

            def link(ins):
                ins.then_inc(done, 1)
                i[0] += 1
                act.wait_ge(done, i[0])

            if LB:
                act.wait_ge(chain, ready["g"])
                link(act.activation(g[:, 5, :], g[:, 0, :], ACT.Sigmoid, scale=-1.0))
                link(act.activation(g[:, 2, :], g[:, 1, :], ACT.Exp, scale=-1.0))
                link(act.activation(g[:, 2, :], g[:, 2, :], ACT.Ln, bias=1.0))
            for c in range(2):
                act.wait_ge(chain, ready["min", c])
                link(act.activation(key[:, c, :], fx[:, c, :], ACT.Sigmoid, scale=-1.0))
                link(act.activation(e[c][:, :], e[c][:, :], ACT.Exp, scale=-1.0))
                link(act.activation(e[c][:, :], e[c][:, :], ACT.Ln, bias=1.0))
                if LB:
                    act.wait_ge(chain, ready["abs2", c])
                    link(act.activation(e[c][:, :], e[c][:, :], ACT.Exp, scale=-1.0))
                    link(act.activation(e[c][:, :], e[c][:, :], ACT.Ln, bias=1.0))
    k.done(sems)


def recurrence(k, direction, q, key, a, v, o, outputs, lay):
    nc, ps, d = k.nc, k.ps, k.d
    X = [lay(f"x{i}", [P, NL, 2, P]) for i in range(2)]
    eq = [lay(f"eq{i}", [P, 2, P]) for i in range(2)]
    qe = [lay(f"qe{i}", [P, 2, P]) for i in range(2)]
    ke = lay("ke", [P, 2, P])
    ket = lay("ket", [P, BR])
    sc = lay("sc", [P, 2, 2, P])
    masks = lay("masks", [P, NL + 1, P])
    S = [lay(f"s{i}", [P, 2, HD]) for i in range(2)]
    order = [0, 1] + list(range(CT_, NT)) if direction == 0 else [1, 0] + list(range(NT - 1, CT_ - 1, -1))
    order = [t for t in order]
    edge = P - 1 if direction == 0 else 0
    query_half = 1 if direction == 0 else 0
    want = [t in outputs for t in order]
    n_out = np.concatenate([[0], np.cumsum(want)]).astype(int).tolist()
    (masks_in, x_exped, subbed, exped, chain, scaled, products, masked, ke_t, ket_out, s_ready, state_out,
     o_ready, o_out) = sems = k.sems(
        "masks_in", "x_exped", "subtracted", "exped", "dve_chain", "scaled", "level_products", "masked",
        "ke_transposed", "ket_out", "state_products", "state_out", "o_ready", "o_out")
    PAIRS = (NL + 1) // 2

    def halves(view, h):
        r = view.rearrange("p c (n s h) -> p c n s h", s=2, h=h)
        return [r[:, :, :, i, :] for i in range(2)]

    with nc.Block() as block:
        @block.sync
        def _(sp):
            sp.dma_start(masks[:, :, :], d["level_masks"][direction]).then_inc(masks_in, 16)
            k.ws.load_until(sp, k.ws.taken)

        @block.gpsimd
        def _(pool):
            for u, t in enumerate(order):
                if not want[u]:
                    continue
                j = n_out[u]
                at = a[:, :, t * P:(t + 1) * P]
                if j >= 2:
                    pool.wait_ge(products, PAIRS * (j - 1))
                for l, h in enumerate(LEVELS):
                    xa, xb = halves(X[j % 2][:, l, :, :], h)
                    aa, ab = halves(at, h)
                    b = aa[:, :, :, h - 1:h] if direction == 0 else ab[:, :, :, 0:1]
                    b = b.to_broadcast([P, 2, P // (2 * h), h])
                    pool.tensor_tensor(xa, *((b, aa) if query_half else (aa, b)), ALU.subtract)
                    ins = pool.tensor_tensor(xb, *((ab, b) if query_half else (b, ab)), ALU.subtract)
                ins.then_inc(subbed, 1)

        @block.scalar
        def _(act):
            for u, t in enumerate(order):
                at = a[:, :, t * P:(t + 1) * P]
                if u >= 2:
                    act.wait_ge(state_out, u - 1)
                act.activation(eq[u % 2][:, :, :], at, ACT.Exp)
                if u >= 1:
                    act.wait_ge(ke_t, u)
                for c in range(2):
                    ins = act.activation(ke[:, c, :], at[:, c, :], ACT.Exp, bias=at[:, c, edge:edge + 1], scale=-1.0)
                ins.then_inc(exped, 1)
                if want[u]:
                    j = n_out[u]
                    act.wait_ge(subbed, j + 1)
                    x = X[j % 2][:, :, :, :]
                    act.activation(x, x, ACT.Exp).then_inc(x_exped, 1)
                act.wait_ge(ke_t, u + 1)
                if u >= 1:
                    act.wait_ge(s_ready, u)
                act.copy(ket[:, :], ps[:, 4, 0:BR]).then_inc(ket_out, 1)

        @block.vector
        def _(dve):
            n = [0]

            def link(ins):
                ins.then_inc(chain, 1)
                n[0] += 1
                dve.wait_ge(chain, n[0])

            dve.memset(sc[:, :, :, :], 0.0)
            link(dve.memset(S[0][:, :, :], 0.0))
            dve.wait_ge(masks_in, 16)

            def scale(u, t):
                qs, ks = q[:, :, t * P:(t + 1) * P], key[:, :, t * P:(t + 1) * P]
                dve.wait_ge(exped, u + 1)
                dve.tensor_tensor(ke[:, :, :], ke[:, :, :], ks, ALU.mult).then_inc(scaled, 1)
                if want[u]:
                    j = n_out[u]
                    if j >= 2:
                        dve.wait_ge(o_ready, j - 1)
                    dve.tensor_tensor(qe[j % 2][:, :, :], eq[u % 2][:, :, :], qs, ALU.mult).then_inc(scaled, 1)
                    dve.wait_ge(x_exped, j + 1)
                    for l, h in enumerate(LEVELS):
                        xh = halves(X[j % 2][:, l, :, :], h)
                        f = [halves(ks, h)[0], halves(qs, h)[1]] if query_half else [halves(qs, h)[0], halves(ks, h)[1]]
                        for i in range(2):
                            ins = dve.tensor_tensor(xh[i], xh[i], f[i], ALU.mult)
                    ins.then_inc(scaled, 1)

            def finish(u, t):
                if want[u]:
                    j = n_out[u]
                    if j >= 1:
                        dve.wait_ge(o_ready, j)
                    for l in range(NL + 1):
                        g, half = PAIRS * j + l // 2, l % 2
                        dve.wait_ge(products, g + 1)
                        if l:
                            dve.wait_ge(masked, (NL + 1) * j + l)
                        b = 2 * (g % 2)
                        dve.copy_predicated(
                            sc[:, :, :, :].rearrange("p a b c -> p (a b) c"),
                            masks[:, l, :].bitcast(U32).unsqueeze(1).to_broadcast([P, 4, P]),
                            ps[:, b:b + 2, half * 256:half * 256 + 256].rearrange("p a (b c) -> p a b c", b=2)
                        ).then_inc(masked, 1)
                dve.wait_ge(s_ready, u + 1)
                for c in range(2):
                    ins = dve.scalar_tensor_tensor(S[(u + 1) % 2][:, c, :], S[u % 2][:, c, :],
                                                   eq[u % 2][:, c, edge:edge + 1],
                                                   ps[:, 5, c * HD:(c + 1) * HD], ALU.mult, ALU.add)
                ins.then_inc(state_out, 1)
                if want[u]:
                    j = n_out[u]
                    dve.wait_ge(o_ready, j + 1)
                    src = ps[:, 6:8, 0:P].rearrange("p a (c e) -> p a c e", c=2)
                    dst = o[:, t, :].rearrange("p (c a e) -> p a c e", c=2, a=2)
                    if direction == 0:
                        dve.tensor_copy(dst, src).then_inc(o_out, 1)
                    else:
                        dve.tensor_tensor(dst, src, dst, ALU.add).then_inc(o_out, 1)
                dve.wait_ge(state_out, u + 1)

            for u, t in enumerate(order):
                scale(u, t)
                if u >= 1:
                    finish(u - 1, order[u - 1])
            finish(len(order) - 1, order[-1])

        @block.tensor
        def _(pe):
            scales = 0
            for u, t in enumerate(order):
                j = n_out[u]
                scales += 1
                pe.wait_ge(scaled, scales)
                if u >= 1:
                    pe.wait_ge(ket_out, u)
                for c in range(2):
                    mm = pe.transpose(ps[:, 4, c * P:(c + 1) * P], ke[:, c, :], k.ident[:, :])
                mm.then_inc(ke_t, 1)
                if want[u]:
                    scales += 2
                    pe.wait_ge(scaled, scales)
                    for l in range(NL + 1):
                        g, half = PAIRS * j + l // 2, l % 2
                        if g >= 2 and half == 0:
                            pe.wait_ge(masked, 2 * (g - 1))
                        for h in range(4):
                            c, par = divmod(h, 2)
                            p0 = par * HD
                            if l < NL:
                                x = X[j % 2][p0:p0 + HD, l, c, :]
                                y = x
                            else:
                                x = key[p0:p0 + HD, c, t * P:(t + 1) * P]
                                y = q[p0:p0 + HD, c, t * P:(t + 1) * P]
                            o0 = half * 256 + c * P
                            mm = pe.matmul(ps[:, 2 * (g % 2) + par, o0:o0 + P], x, y, start=True, stop=True)
                        if half:
                            mm.then_inc(products, 1)
                pe.wait_ge(ket_out, u + 1)
                if u >= 1:
                    pe.wait_ge(state_out, u)
                for h in range(4):
                    c, p0 = h // 2, (h % 2) * HD
                    mm = pe.matmul(ps[p0:p0 + HD, 5, c * HD:(c + 1) * HD], ket[:, h * HD:(h + 1) * HD],
                                   v[:, t, h * HD:(h + 1) * HD], start=True, stop=True)
                mm.then_inc(s_ready, 1)
                if want[u]:
                    if j >= 1:
                        pe.wait_ge(o_out, j)
                    pe.wait_ge(masked, (NL + 1) * (j + 1))
                    for h in range(4):
                        c, p0 = h // 2, (h % 2) * HD
                        out = ps[:, 6 + h % 2, c * HD:(c + 1) * HD]
                        pe.matmul(out, sc[:, h % 2, c, :], v[:, t, h * HD:(h + 1) * HD], start=True, stop=False)
                        mm = pe.matmul(out, qe[j % 2][p0:p0 + HD, c, :], S[u % 2][p0:p0 + HD, c, :], start=False, stop=True)
                    mm.then_inc(o_ready, 1)
    k.done(sems)


def recurrence_norm(k, layer, o, yt, t_from, lay):
    nc, ps, d = k.nc, k.ps, k.d
    sq = lay("sq", [P, 2, BR])
    stat = lay("stat", [P, NT, 4])
    gain = lay("gain", [P, 2])
    gain_in, chain, mean_done, rooted, transposed, evacuated = sems = k.sems(
        "gain_in", "dve_chain", "mean_done", "rooted", "transposed", "evacuated")
    k_scaled = [0]
    groups = [(0, 2), (2, 4), (6, 4)] if t_from == 0 else [(2, 4), (6, 4)]
    with nc.Block() as block:
        @block.sync
        def _(sp):
            sp.dma_start(gain[:, :], d["hgrn_norm_g"][layer].rearrange("(c p) -> p c", p=P)).then_inc(gain_in, 16)
            k.ws.load_until(sp, k.ws.taken)

        @block.vector
        def _(dve):
            n = [0]

            def link(ins):
                ins.then_inc(chain, 1)
                n[0] += 1
                dve.wait_ge(chain, n[0])

            for t in range(t_from, NT):
                s = sq[:, t % 2, :].rearrange("p (h e) -> p h e", h=4)
                link(dve.tensor_tensor(sq[:, t % 2, :], o[:, t, :], o[:, t, :], ALU.mult))
                link(dve.tensor_reduce(stat[:, t, :], s, AX.X, ALU.add))
            st = stat[:, t_from:NT, :]
            dve.tensor_scalar(st, st, 1.0 / HD, EPS, ALU.mult, ALU.add).then_inc(mean_done, 1)
            dve.wait_ge(rooted, 1)
            link(dve.reciprocal(st, st))
            for t in range(t_from, NT):
                ot = o[:, t, :].rearrange("p (h e) -> p h e", h=4)
                link(dve.tensor_tensor(ot, ot, stat[:, t, :].unsqueeze(2).to_broadcast([P, 4, HD]), ALU.mult))
            k_scaled[0] = n[0]
            dve.wait_ge(gain_in, 16)
            for g, (t0, tn) in enumerate(groups):
                for c in range(2):
                    y = yt[:, 4 + c, t0 * P:(t0 + tn) * P]
                    dve.wait_ge(transposed, 2 * g + c + 1)
                    dve.scalar_tensor_tensor(y, ps[:, 2 * g + c, 0:tn * P], gain[:, c:c + 1], y,
                                             ALU.mult, ALU.mult).then_inc(evacuated, 1)

        @block.scalar
        def _(act):
            st = stat[:, t_from:NT, :]
            act.wait_ge(mean_done, 1)
            act.activation(st, st, ACT.Sqrt).then_inc(rooted, 1)

        @block.tensor
        def _(pe):
            pe.wait_ge(chain, k_scaled[0])
            for g, (t0, tn) in enumerate(groups):
                for c in range(2):
                    for i in range(tn):
                        mm = pe.transpose(ps[:, 2 * g + c, i * P:(i + 1) * P], o[:, t0 + i, c * P:(c + 1) * P],
                                          k.ident[:, :])
                    mm.then_inc(transposed, 1)
    k.done(sems)


def fourier_channels(k, fu, z, lay):
    nc, ps, d = k.nc, k.ps, k.d
    tab = lay("channel_dft", [P, 2, P])
    tab_in, ready, out_act, out_dve = sems = k.sems("table_in", "ready", "out_act", "out_dve")
    with nc.Block() as block:
        @block.sync
        def _(sp):
            sp.dma_start(tab[:, :, :], d["dft_channels"]).then_inc(tab_in, 16)
            k.ws.load_until(sp, k.ws.taken)

        @block.tensor
        def _(pe):
            pe.wait_ge(tab_in, 16)
            for t in range(NT):
                if t >= 4:
                    pe.wait_ge(out_act, t - 3)
                    pe.wait_ge(out_dve, t - 3)
                for c in range(2):
                    pe.matmul(ps[:, 2 * (t % 4) + c, 0:2 * P], fu[:, c, t * P:(t + 1) * P], tab[:, :, :],
                              start=True, stop=True).then_inc(ready, 1)

        @block.scalar
        def _(act):
            for t in range(NT):
                act.wait_ge(ready, 2 * t + 1)
                act.copy(z[:, t, :, 0:P], ps[:, 2 * (t % 4), 0:2 * P].rearrange("p (a b) -> p a b", a=2)
                         ).then_inc(out_act, 1)

        @block.vector
        def _(dve):
            for t in range(NT):
                dve.wait_ge(ready, 2 * t + 2)
                dve.tensor_copy(z[:, t, :, P:2 * P], ps[:, 2 * (t % 4) + 1, 0:2 * P].rearrange("p (a b) -> p a b", a=2)
                                ).then_inc(out_dve, 1)
    k.done(sems)


def mixer_layer(k, layer, XT, YT):
    ctx_out = layer == 0
    nt0 = 0 if ctx_out else CT_
    blocks = ALL_BLOCKS if ctx_out else LAT_BLOCKS
    tiles = [(t * P, P) for t in range(nt0, NT)]
    all_tiles = [(t * P, P) for t in range(NT)]

    def x(kx, t0, tn):
        return XT[:, kx, t0:t0 + tn]

    def fm(cols, dst, do, toks, ct0=0):
        return dict(mode="fm", x=x, kt=KD, cols=cols, toks=toks, do=do,
                    dst=lambda s, n: dst(s + ct0)[:, toks[n][0]:toks[n][0] + toks[n][1]])

    def tm(cols, dst, do, toks):
        return dict(mode="tm", x=x, kt=KD, cols=cols, toks=toks, do=do, dst=dst)

    lay = Layout(k, A_R, A_C - 1024)
    parts = [lay(n, [P, 2, T]) for n in ("cb", "cc", "cv", "cz")]
    def conv_dst(i):
        return lambda s: parts[i + s // 2][:, s % 2, :]
    project(k, [fm(HALF, conv_dst(0), "copy", ALL_BLOCKS),
                dict(fm(HALF, conv_dst(2), "copy", ALL_BLOCKS), silu_from=2)])
    conv_branch(k, layer, [p for p in parts], YT)

    lay = Layout(k, A_R, A_C)
    qt, kt = lay("qt", [P, 4, T]), lay("kt", [P, 2, T])
    v = lay("v", [P, NT, 2, 3 * HD])
    scratch = lay.o
    qkv = lay("qkv", [P, NT, HALF])
    project(k, [tm(HALF, lambda s, n: qkv[:, n, :], "copy", all_tiles),
                fm(BR, lambda c: YT[:, 2 + c, :], "silu", ALL_BLOCKS)])
    heads_prepare(k, layer, qkv, qt, kt, v, lay)
    units = []
    for h in range(4):
        g = h // 2
        for t0, tn in blocks:
            nk, s0 = (CTX, 0) if t0 == 0 else (T, 0)
            units.append(dict(
                rows=(0, HD), rows_max=(0, HD + 1), row=HD, odd=h % 2, nq=tn, nk=nk,
                q=qt[:, h, t0:t0 + tn], k=kt[:, g, s0:s0 + nk],
                v=(lambda i, g=g, h=h: v[:, i, g, (h % 2) * HD:(h % 2) * HD + P]),
                out=YT[(h % 2) * HD:(h % 2 + 1) * HD, 2 + g, t0:t0 + tn]))
    attention(k, units, Layout(k, scratch, A_C), HD ** -0.5, True)

    lay = Layout(k, A_R, A_C)
    q, a, key = (lay(n, [P, 2, T]) for n in ("q", "a", "key"))
    v, o = lay("v", [P, NT, BR]), lay("o", [P, NT, BR])
    project(k, [fm(BR, lambda c: q[:, c, :], "silu", ALL_BLOCKS),
                tm(BR, lambda s, n: v[:, n, :], "copy", all_tiles),
                fm(BR, lambda c: YT[:, 4 + c, :], "silu", ALL_BLOCKS)])
    for direction in range(2):
        project(k, [fm(BR, lambda c: a[:, c, :], "copy", ALL_BLOCKS)])
        recurrence_gates(k, layer, direction, a, key, Layout(k, lay.o, A_C))
        recurrence(k, direction, q, key, a, v, o, range(nt0, NT), Layout(k, lay.o, A_C))
    recurrence_norm(k, layer, o, YT, nt0, Layout(k, lay.o, A_C))

    lay = Layout(k, A_R, A_C)
    fu, z = lay("fu", [P, 2, T]), lay("z", [P, NT, 2, BR])
    project(k, [fm(BR, lambda c: fu[:, c, :], "copy", ALL_BLOCKS),
                fm(BR, lambda c: YT[:, 6 + c, :], "silu", ALL_BLOCKS)])
    fourier_channels(k, fu, z, lay)

    def spectrum(cols, kt, tile0, n_tiles, t_out):
        return dict(mode="tm", kt=2 * n_tiles, cols=cols, toks=[(0, P), (P, P)], do="mul",
                    x=lambda kx, t0, tn: z[:, tile0 + kx % n_tiles, kx // n_tiles, t0:t0 + tn],
                    dst=lambda s, n: YT[:, 6 + n, t_out:t_out + cols])
    jobs = []
    if ctx_out:
        jobs.append(spectrum(CTX, 4, 0, CT_, 0))
    for b in range(2):
        jobs.append(spectrum(HALF, 16, CT_, LAT // P, CTX + b * HALF))
    project(k, jobs)

    out = k.at("branch_out", [P, NT, D], A_A if XT is k.buf[0] else A_B)
    project(k, [dict(mode="tm", kt=KD, cols=HALF, toks=tiles, do="copy",
                     x=lambda kx, t0, tn: YT[:, kx, t0:t0 + tn],
                     dst=lambda s, n, b=b: out[:, nt0 + n, b * HALF:(b + 1) * HALF]) for b in range(2)])
    return out


def latents_prepare(k, raw, cqT, ckvT, krT, lay, lay2):
    nc, ps, d = k.nc, k.ps, k.d
    junk = lay("junk", [P, QL])
    stat = lay("stat", [P, NT, 2])
    cs = lay2("rope_tables", [P, 2, LAT // P, RD])
    t1 = lay("t1", [P, LAT // P, RD])
    t2 = lay("t2", [P, LAT // P, RD])
    gq, gkv = lay("gq", [P, 3]), lay("gkv", [P, 2])
    (in_, squared, mean_done, rooted, chain, scaled, transposed, out_act, out_dve) = sems = k.sems(
        "tables_in", "squared", "mean_done", "rooted", "dve_chain", "scaled", "transposed", "out_act", "out_dve")
    with nc.Block() as block:
        @block.sync
        def _(sp):
            sp.dma_start(cs[:, 0, :, :], d["rope2_tm"][0].rearrange("(t p) f -> p t f", p=P)).then_inc(in_, 16)
            sp.dma_start(cs[:, 1, :, :], d["rope2_tm"][1].rearrange("(t p) f -> p t f", p=P)).then_inc(in_, 16)
            sp.dma_start(gq[:, :], d["q_norm_2"][0].rearrange("(c p) -> p c", p=P)).then_inc(in_, 16)
            sp.dma_start(gkv[:, :], d["kv_norm_2"][0].rearrange("(c p) -> p c", p=P)).then_inc(in_, 16)
            k.ws.load_until(sp, k.ws.taken)

        @block.scalar
        def _(act):
            for t in range(NT):
                act.activation(junk[:, 0:QL], raw[:, t, 0:QL], ACT.Square, scale=(1.0 / QL) ** 0.5,
                               accum_out=stat[:, t, 0:1]).then_inc(squared, 1)
                act.wait_ge(squared, 2 * t + 1)
                act.activation(junk[:, 0:KVL], raw[:, t, QL:QL + KVL], ACT.Square, scale=(1.0 / KVL) ** 0.5,
                               accum_out=stat[:, t, 1:2]).then_inc(squared, 1)
                act.wait_ge(squared, 2 * t + 2)
            act.wait_ge(mean_done, 1)
            act.activation(stat[:, :, :], stat[:, :, :], ACT.Sqrt).then_inc(rooted, 1)
            act.wait_ge(in_, 64)
            for t in range(CT_, NT):
                act.wait_ge(transposed, t + 1)
                for c in range(3):
                    ins = act.activation(cqT[:, c, (t - CT_) * P:(t - CT_ + 1) * P], ps[:, 2 * (t % 2), c * P:(c + 1) * P],
                                         ACT.Copy, scale=gq[:, c:c + 1])
                ins.then_inc(out_act, 1)

        @block.vector
        def _(dve):
            n = [0]

            def link(ins):
                ins.then_inc(chain, 1)
                n[0] += 1
                dve.wait_ge(chain, n[0])

            dve.wait_ge(in_, 64)
            kr = raw[:, CT_:NT, QL + KVL:]
            link(dve.tensor_tensor(t1[:, :, :], kr, cs[:, 0, :, :], ALU.mult))
            for ax in range(2):
                for half in range(2):
                    o, i = 16 * ax + 8 * half, 16 * ax + 8 * (1 - half)
                    dve.tensor_tensor(t2[:, :, o:o + 8], kr[:, :, i:i + 8], cs[:, 1, :, o:o + 8],
                                      ALU.mult).then_inc(chain, 1)
                    n[0] += 1
            dve.wait_ge(chain, n[0])
            link(dve.tensor_tensor(kr, t1[:, :, :], t2[:, :, :], ALU.add))
            dve.wait_ge(squared, 2 * NT)
            dve.tensor_scalar(stat[:, :, :], stat[:, :, :], EPS, None, ALU.add).then_inc(mean_done, 1)
            dve.wait_ge(rooted, 1)
            link(dve.reciprocal(stat[:, :, :], stat[:, :, :]))

            def out(t):
                dve.wait_ge(transposed, t + 1)
                for c in range(2):
                    dve.tensor_scalar(ckvT[:, c, t * P:(t + 1) * P], ps[:, 2 * (t % 2) + 1, c * P:(c + 1) * P],
                                      gkv[:, c:c + 1], None, ALU.mult)
                dve.tensor_copy(krT[0:RD, t * P:(t + 1) * P], ps[0:RD, 2 * (t % 2) + 1, 2 * P:3 * P]).then_inc(out_dve, 1)

            for t in range(NT):
                dve.tensor_scalar(raw[:, t, 0:QL], raw[:, t, 0:QL], stat[:, t, 0:1], None, ALU.mult)
                dve.tensor_scalar(raw[:, t, QL:QL + KVL], raw[:, t, QL:QL + KVL], stat[:, t, 1:2], None,
                                  ALU.mult).then_inc(scaled, 1)
                if t >= 1:
                    out(t - 1)
            out(NT - 1)

        @block.tensor
        def _(pe):
            for t in range(NT):
                pe.wait_ge(scaled, t + 1)
                if t >= 2:
                    pe.wait_ge(out_dve, t - 1)
                if t - 2 >= CT_:
                    pe.wait_ge(out_act, t - 2 - CT_ + 1)
                if t >= CT_:
                    for c in range(3):
                        pe.transpose(ps[:, 2 * (t % 2), c * P:(c + 1) * P], raw[:, t, c * P:(c + 1) * P], k.ident[:, :])
                for c in range(2):
                    o = QL + c * P
                    pe.transpose(ps[:, 2 * (t % 2) + 1, c * P:(c + 1) * P], raw[:, t, o:o + P], k.ident[:, :])
                pe.transpose(ps[0:RD, 2 * (t % 2) + 1, 2 * P:3 * P], raw[:, t, QL + KVL:], k.ident[:, :]
                             ).then_inc(transposed, 1)
    k.done(sems)


def query_rope(k, cqT, qr, lay, lay2):
    nc, ps, d = k.nc, k.ps, k.d
    w = [lay(f"wqr{i}", [P, 3, P]) for i in range(2)]
    tab = lay2("rope_fm", [P, 2, LAT])
    t1 = lay("t1", [P, HALF])
    t2 = lay("t2", [P, HALF])
    tab_in, w_in0, w_in1, ready, used, done, chain = sems = k.sems(
        "tables_in", "w_plain_in", "w_swapped_in", "ready", "w_used", "turned", "dve_chain")
    with nc.Block() as block:
        @block.sync
        def _(sp):
            for i in range(2):
                sp.dma_start(tab[:, i, :], d["rope2_fm"][i]).then_inc(tab_in, 16)
            for g in range(4):
                for i, s in enumerate((w_in0, w_in1)):
                    if g >= 1:
                        sp.wait_ge(ready, 4 * g)
                    sp.dma_start(w[i][:, :, :], d[("wq_rope", "wq_rope_sw")[i]][:, g * P:(g + 1) * P].rearrange(
                        "(c p) n -> p c n", p=P)).then_inc(s, 16)
            k.ws.load_until(sp, k.ws.taken)

        @block.tensor
        def _(pe):
            for g in range(4):
                pe.wait_ge(w_in0, 16 * (g + 1))
                pe.wait_ge(w_in1, 16 * (g + 1))
                for b in range(2):
                    j = 2 * g + b
                    if j >= 2:
                        pe.wait_ge(done, j - 1)
                    for i in range(2):
                        for c in range(3):
                            mm = pe.matmul(ps[:, 2 * (j % 2) + i, :], w[i][:, c, :], cqT[:, c, b * HALF:(b + 1) * HALF],
                                           start=(c == 0), stop=(c == 2))
                        mm.then_inc(ready, 1)

        @block.vector
        def _(dve):
            dve.wait_ge(tab_in, 32)
            for g in range(4):
                for b in range(2):
                    j = 2 * g + b
                    cols = slice(b * HALF, (b + 1) * HALF)
                    dve.wait_ge(ready, 2 * j + 2)
                    dve.tensor_tensor(t1[:, :], ps[:, 2 * (j % 2), :], tab[:, 0, cols], ALU.mult).then_inc(chain, 1)
                    dve.tensor_tensor(t2[:, :], ps[:, 2 * (j % 2) + 1, :], tab[:, 1, cols], ALU.mult).then_inc(chain, 1)
                    dve.wait_ge(chain, 2 * j + 2)
                    dve.tensor_tensor(qr[:, g, cols], t1[:, :], t2[:, :], ALU.add).then_inc(done, 1)
                    dve.wait_ge(done, j + 1)
    k.done(sems)


def pair_projections(k, p, cqT, ckvT, krT, qr, Q, Kt, V, wts):
    nc, ps, d = k.nc, k.ps, k.d
    wq, wk, wv = wts
    (w_in, q_ready, k_ready, v_ready, out_act, out_dve) = sems = k.sems(
        "weights_in", "q_ready", "k_ready", "v_ready", "out_act", "out_dve")
    with nc.Block() as block:
        @block.sync
        def _(sp):
            for dst, src in ((wq, "wq_nope"), (wk, "wk_nope"), (wv, "wv")):
                sp.dma_start(dst[:, :, :], d[src][:, p * P:(p + 1) * P].rearrange("(c p) n -> p c n", p=P)
                             ).then_inc(w_in, 16)
            k.ws.load_until(sp, k.ws.taken)

        @block.tensor
        def _(pe):
            pe.wait_ge(w_in, 48)
            for b in range(2):
                for c in range(3):
                    mm = pe.matmul(ps[:, b, :], wq[:, c, :], cqT[:, c, b * HALF:(b + 1) * HALF],
                                   start=(c == 0), stop=(c == 2))
                mm.then_inc(q_ready, 1)
            for b, (t0, tn) in enumerate(ALL_BLOCKS):
                for c in range(2):
                    mm = pe.matmul(ps[:, 2 + b, 0:tn], wk[:, c, :], ckvT[:, c, t0:t0 + tn],
                                   start=(c == 0), stop=(c == 1))
                mm.then_inc(k_ready, 1)
            for t in range(NT):
                for c in range(2):
                    mm = pe.matmul(ps[:, 5 + t // 4, (t % 4) * P:(t % 4 + 1) * P], ckvT[:, c, t * P:(t + 1) * P],
                                   wv[:, c, :], start=(c == 0), stop=(c == 1))
                if t % 4 == 3 or t == NT - 1:
                    mm.then_inc(v_ready, 1)

        @block.scalar
        def _(act):
            for b in range(2):
                act.wait_ge(q_ready, b + 1)
                act.copy(Q[0][0:64, b * HALF:(b + 1) * HALF], ps[0:64, b, :])
                act.copy(Q[1][64:128, b * HALF:(b + 1) * HALF], ps[64:128, b, :])
            for b, (t0, tn) in enumerate(ALL_BLOCKS[:2]):
                act.wait_ge(k_ready, b + 1)
                act.copy(Kt[0][0:64, t0:t0 + tn], ps[0:64, 2 + b, 0:tn])
                act.copy(Kt[1][64:128, t0:t0 + tn], ps[64:128, 2 + b, 0:tn])

        @block.vector
        def _(dve):
            h = 2 * p
            dve.memset(Q[1][32:64, :], 0.0)
            dve.tensor_copy(Q[0][64:96, :], qr[32 * (h % 4):32 * (h % 4) + 32, h // 4, :])
            dve.tensor_copy(Q[1][0:32, :], qr[32 * (h % 4) + 32:32 * (h % 4) + 64, h // 4, :])
            if p == 0:
                dve.tensor_copy(Kt[0][64:96, :], krT[0:RD, :])
                dve.tensor_copy(Kt[1][0:32, :], krT[0:RD, :])
                dve.memset(Kt[0][96:97, :], 1.0)
                dve.memset(V[:, :, 64:128], 1.0)
                dve.memset(Kt[1][32:64, :], 0.0).then_inc(out_dve, 1)
                dve.wait_ge(out_dve, 1)
                dve.memset(Kt[1][32:33, :], 1.0)
            t0, tn = ALL_BLOCKS[2]
            dve.wait_ge(k_ready, 3)
            dve.tensor_copy(Kt[0][0:64, t0:t0 + tn], ps[0:64, 4, 0:tn])
            dve.tensor_copy(Kt[1][64:128, t0:t0 + tn], ps[64:128, 4, 0:tn])
            for g in range(3):
                n = min(4, NT - 4 * g)
                dve.wait_ge(v_ready, g + 1)
                src = ps[:, 5 + g, 0:n * P].rearrange("p (t c) -> p t c", c=P)
                dve.tensor_copy(V[:, 4 * g:4 * g + n, 0:64], src[:, :, 0:64])
                dve.tensor_copy(V[:, 4 * g:4 * g + n, 128:192], src[:, :, 64:128])
    k.done(sems)


def spill(k, moves):
    (moved,) = sems = k.sems("moved")
    with k.nc.Block() as block:
        @block.sync
        def _(sp):
            for dst, src in moves:
                sp.dma_start(dst, src).then_inc(moved, 16)
            sp.wait_ge(moved, 16 * len(moves))
            k.ws.load_until(sp, k.ws.taken)


def ssd_conv(k, j0, raw, conv, xs, bt, ct, btm, lay):
    nc, ps, d = k.nc, k.ps, k.d
    taps = lay("taps", [P, 6, 4])
    taps_in, chain, convolved, activated, transposed, out_act, out_dve = sems = k.sems(
        "taps_in", "dve_chain", "convolved", "activated", "transposed", "out_act", "out_dve")
    groups = [(0, 4), (4, 4), (8, 2)]
    turned = [j for j in range(4) if j0 + j < 10]

    def place(j):
        g = j0 + j
        return bt[:, g - 8, :] if g in (8, 9) else ct[:, g - 10, :] if g >= 10 else raw[:, j, :]

    def tm_place(j, t0, tn):
        g = j0 + j
        if g < 8:
            return xs[:, t0:t0 + tn, g * P:(g + 1) * P]
        return btm[:, t0:t0 + tn, (g - 8) * P:(g - 7) * P]

    with nc.Block() as block:
        @block.sync
        def _(sp):
            for i in range(5):
                sp.dma_start(taps[:, i, :], d["ssd_conv_w_2"][0, i, j0 * P:(j0 + 4) * P].rearrange("(c p) -> p c", p=P)
                             ).then_inc(taps_in, 16)
            sp.dma_start(taps[:, 5, :], d["ssd_conv_b_2"][0, j0 * P:(j0 + 4) * P].rearrange("(c p) -> p c", p=P)
                         ).then_inc(taps_in, 16)
            k.ws.load_until(sp, k.ws.taken)

        @block.vector
        def _(dve):
            n = [0]

            def link(ins):
                ins.then_inc(chain, 1)
                n[0] += 1
                dve.wait_ge(chain, n[0])

            dve.wait_ge(taps_in, 96)
            for j in range(4):
                x, y = raw[:, j, :], conv[:, j, :]
                link(dve.tensor_scalar(y, x, taps[:, 2, j:j + 1], taps[:, 5, j:j + 1], ALU.mult, ALU.add))
                for i in (0, 1, 3, 4):
                    s = i - 2
                    for a, b in ((0, CTX), (CTX, T)):
                        lo, hi = max(a, a - s), min(b, b - s)
                        ins = dve.scalar_tensor_tensor(y[:, lo:hi], x[:, lo + s:hi + s], taps[:, i, j:j + 1],
                                                       y[:, lo:hi], ALU.mult, ALU.add)
                        if (i, a) != (4, CTX):
                            link(ins)
                ins.then_inc(convolved, 1)
            for i, j in enumerate(turned):
                for g, (t0, tn) in enumerate(groups):
                    if (3 * i + g) % 2:
                        continue
                    m = 3 * i + g
                    dve.wait_ge(transposed, m + 1)
                    dve.tensor_copy(tm_place(j, t0, tn), ps[:, m % 8, 0:tn * P].rearrange("p (t c) -> p t c", c=P)
                                    ).then_inc(out_dve, 1)

        @block.scalar
        def _(act):
            for j in range(4):
                act.wait_ge(convolved, j + 1)
                act.activation(place(j), conv[:, j, :], ACT.Silu).then_inc(activated, 1)
            for i, j in enumerate(turned):
                for g, (t0, tn) in enumerate(groups):
                    m = 3 * i + g
                    if m % 2 == 0:
                        continue
                    act.wait_ge(transposed, m + 1)
                    act.copy(tm_place(j, t0, tn), ps[:, m % 8, 0:tn * P].rearrange("p (t c) -> p t c", c=P)
                             ).then_inc(out_act, 1)

        @block.tensor
        def _(pe):
            for i, j in enumerate(turned):
                pe.wait_ge(activated, j + 1)
                for g, (t0, tn) in enumerate(groups):
                    m = 3 * i + g
                    if m >= 8:
                        pe.wait_ge(out_act if (m - 8) % 2 else out_dve, (m - 8) // 2 + 1)
                    for t in range(tn):
                        mm = pe.transpose(ps[:, m % 8, t * P:(t + 1) * P], place(j)[:, (t0 + t) * P:(t0 + t + 1) * P],
                                          k.ident[:, :])
                    mm.then_inc(transposed, 1)
    k.done(sems)


ND = 32


def ssd_decays(k, dt, w_end, tot, eac, ac, dta, tri, skip, lay):
    nc, ps, d = k.nc, k.ps, k.d
    N = NT * ND
    bias, alog = lay("bias", [P, ND]), lay("alog", [P, ND])
    t1, t2 = lay("t1", [P, NT, ND]), lay("t2", [P, NT, ND])
    ones = lay("ones", [P, P])
    in_, chain, acts, sums = sems = k.sems("rows_in", "dve_chain", "act_done", "sums")
    mark = {}
    with nc.Block() as block:
        @block.vector
        def _(dve):
            n = [0]

            def link(ins):
                ins.then_inc(chain, 1)
                n[0] += 1
                dve.wait_ge(chain, n[0])
                return n[0]

            def over_tiles(row):
                return row[:, :].unsqueeze(1).to_broadcast([P, NT, ND])

            link(dve.memset(ones[:, :], 1.0))
            dve.wait_ge(in_, 64)
            link(dve.tensor_tensor(dt[:, :, :], dt[:, :, :], over_tiles(bias), ALU.add))
            mark["abs"] = link(dve.scalar_tensor_tensor(t1[:, :, :], dt[:, :, :], -1.0, dt[:, :, :], ALU.mult, ALU.max))
            link(dve.tensor_scalar(dt[:, :, :], dt[:, :, :], 0.0, None, ALU.max))
            dve.wait_ge(acts, 3)
            link(dve.tensor_tensor(dt[:, :, :], dt[:, :, :], t1[:, :, :], ALU.add))
            link(dve.tensor_tensor(dta[:, :, :], dt[:, :, :], over_tiles(alog), ALU.mult))
            mark["dta"] = link(dve.tensor_scalar(dta[:, :, :], dta[:, :, :], -1.0, None, ALU.mult))
            dve.wait_ge(sums, 2)
            link(dve.tensor_copy(ac[:, :, :], ps[:, 0, 0:N].rearrange("p (t c) -> p t c", t=NT)))
            mark["end"] = link(dve.tensor_tensor(t2[:, :, :], ps[:, 1, 0:N].rearrange("p (t c) -> p t c", t=NT),
                                                 ac[:, :, :], ALU.subtract))
            dve.wait_ge(acts, 6)
            dve.tensor_tensor(w_end[:, :, :], dt[:, :, :], t2[:, :, :], ALU.mult)

        @block.sync
        def _(sp):
            sp.dma_start(bias[:, :], d["ssd_dt_bias_2"].rearrange("a b c -> a (b c)").to_broadcast([P, ND])).then_inc(in_, 16)
            sp.dma_start(alog[:, :], d["ssd_a_log_2"].rearrange("a b c -> a (b c)").to_broadcast([P, ND])).then_inc(in_, 16)
            sp.dma_start(tri[:, :, :], d["tri"]).then_inc(in_, 16)
            sp.dma_start(skip[:, :], d["ssd_d_2"][0:1, :].to_broadcast([P, NH2])).then_inc(in_, 16)
            k.ws.load_until(sp, k.ws.taken)

        @block.scalar
        def _(act):
            act.wait_ge(in_, 64)
            act.activation(alog[:, :], alog[:, :], ACT.Exp).then_inc(acts, 1)
            act.wait_ge(chain, mark["abs"])
            act.activation(t1[:, :, :], t1[:, :, :], ACT.Exp, scale=-1.0).then_inc(acts, 1)
            act.wait_ge(acts, 2)
            act.activation(t1[:, :, :], t1[:, :, :], ACT.Ln, bias=1.0).then_inc(acts, 1)
            act.wait_ge(chain, mark["end"])
            act.activation(eac[:, :, :], ac[:, :, :], ACT.Exp).then_inc(acts, 1)
            act.activation(tot[:, :, :], ps[:, 1, 0:N].rearrange("p (t c) -> p t c", t=NT), ACT.Exp).then_inc(acts, 1)
            act.activation(t2[:, :, :], t2[:, :, :], ACT.Exp).then_inc(acts, 1)

        @block.tensor
        def _(pe):
            pe.wait_ge(chain, mark["dta"])
            for t in range(NT):
                for dr in range(2):
                    mm = pe.matmul(ps[:, 0, t * ND + 16 * dr:t * ND + 16 * dr + 16], tri[:, dr, :],
                                   dta[:, t, 16 * dr:16 * dr + 16], start=True, stop=True)
            mm.then_inc(sums, 1)
            pe.matmul(ps[:, 1, 0:N], ones[:, :], dta[:, :, :].rearrange("p t c -> p (t c)"), start=True, stop=True
                      ).then_inc(sums, 1)
    k.done(sems)


def ssd_scan(k, direction, xs, bt, ct, btm, dt, dta, tri, w_end, tot, eac, ac, y, skip, lay):
    nc, ps, d = k.nc, k.ps, k.d
    order = [0, 1] + list(range(CT_, NT)) if direction == 0 else [1, 0] + list(range(NT - 1, CT_ - 1, -1))
    xw = [lay(f"xw{i}", [P, D]) for i in range(2)]
    S = [lay(f"s{i}", [P, D]) for i in range(2)]
    tmp = lay("tmp", [P, HALF])
    if direction == 0:
        xd = [lay(f"xd{i}", [P, D]) for i in range(2)]
        cb = lay("cb", [P, 2, P])
        E = [lay(f"e{i}", [P, 4, P]) for i in range(2)]
    H8 = 8
    (weighted, chain, off_ready, inc_ready, state_out, cb_ready, cb_out, a_ready, capped, exped, w_ready,
     diag_done, y_out) = sems = k.sems(
        "weighted", "dve_chain", "off_ready", "state_products", "state_out", "cb_ready", "cb_out", "a_ready",
        "capped", "exped", "w_ready", "diag_done", "y_out")
    dr = direction
    lat_units = [u for u, t in enumerate(order) if t >= CT_]

    def per_head(view, t, g, which):
        return view[:, t, 16 * which + H8 * g:16 * which + H8 * (g + 1)].unsqueeze(2).to_broadcast([P, H8, HD])

    def heads(view):
        return view.rearrange("p (h e) -> p h e", h=H8)

    def quad(i, g, w, q):
        return ((i * 2 + g) * 2 + w) * 2 + q

    with nc.Block() as block:
        @block.sync
        def _(sp):
            k.ws.load_until(sp, k.ws.taken)

        @block.gpsimd
        def _(pool):
            for u, t in enumerate(order):
                if u >= 2:
                    pool.wait_ge(inc_ready, 2 * (u - 1))
                for g in range(2):
                    sl = slice(g * HALF, (g + 1) * HALF)
                    ins = pool.tensor_tensor(heads(xw[u % 2][:, sl]), heads(xs[:, t, sl]), per_head(w_end, t, g, dr),
                                             ALU.mult)
                if dr == 0 and t >= CT_:
                    i = u - CT_
                    if i >= 1:
                        pool.wait_ge(diag_done, 8 * i)
                    for w in range(2):
                        for g in range(2):
                            sl = slice(g * HALF, (g + 1) * HALF)
                            ins = pool.tensor_tensor(heads(xd[w][:, sl]), heads(xs[:, t, sl]), per_head(dt, t, g, w),
                                                     ALU.mult)
                ins.then_inc(weighted, 1)

        @block.tensor
        def _(pe):
            for u, t in enumerate(order):
                tok = slice(t * P, (t + 1) * P)
                i = u - CT_
                pe.wait_ge(weighted, u + 1)
                pe.wait_ge(state_out, 2 * u + 2)
                if t >= CT_:
                    for g in range(2):
                        if i >= 1:
                            pe.wait_ge(y_out, (2 * i if dr else 4 * i))
                        pe.matmul(ps[:, g, :], ct[:, g, tok], S[u % 2][:, g * HALF:(g + 1) * HALF],
                                  start=True, stop=True).then_inc(off_ready, 1)
                for g in range(2):
                    pe.matmul(ps[:, 2 + g, :], btm[:, t, g * P:(g + 1) * P], xw[u % 2][:, g * HALF:(g + 1) * HALF],
                              start=True, stop=True).then_inc(inc_ready, 1)
                if dr == 0 and t >= CT_:
                    for g in range(2):
                        j = 2 * i + g
                        if j >= 1:
                            pe.wait_ge(cb_out, j)
                        pe.matmul(ps[:, 4, 0:P], bt[:, g, tok], ct[:, g, tok], start=True, stop=True).then_inc(cb_ready, 1)

                        def sums(m):
                            w, q = divmod(m, 2)
                            n = quad(i, g, w, q)
                            if n >= 2:
                                pe.wait_ge(capped, n - 1)
                            for h in range(4):
                                c = 16 * w + H8 * g + 4 * q + h
                                mm = pe.matmul(ps[:, 5 + n % 2, h * P:(h + 1) * P],
                                               dta[:, t, c:c + 1].to_broadcast([P, P]), tri[:, w, :],
                                               start=True, stop=True)
                            mm.then_inc(a_ready, 1)

                        def diag(m):
                            w, q = divmod(m, 2)
                            n = quad(i, g, w, q)
                            pe.wait_ge(w_ready, n + 1)
                            if n % 4 == 0 and j >= 1:
                                pe.wait_ge(y_out, 4 * i + 3 * g)
                            for h in range(4):
                                hh = 4 * q + h
                                mm = pe.matmul(ps[:, 7, hh * HD:(hh + 1) * HD], E[n % 2][:, h, :],
                                               xd[w][:, g * HALF + hh * HD:g * HALF + (hh + 1) * HD],
                                               start=(m == 0 and h == 0), stop=(w == 1), skip_group_check=True)
                            mm.then_inc(diag_done, 1)

                        sums(0)
                        sums(1)
                        for m in range(4):
                            diag(m)
                            if m + 2 < 4:
                                sums(m + 2)

        @block.vector
        def _(dve):
            n = [0]

            def link(ins):
                ins.then_inc(chain, 1)
                n[0] += 1
                dve.wait_ge(chain, n[0])

            for g in range(2):
                dve.memset(S[0][:, g * HALF:(g + 1) * HALF], 0.0).then_inc(state_out, 1)
            dve.wait_ge(state_out, 2)
            for u, t in enumerate(order):
                i = u - CT_
                for g in range(2):
                    sl = slice(g * HALF, (g + 1) * HALF)
                    if t >= CT_:
                        yt = y[:, t - CT_, sl]
                        dve.wait_ge(off_ready, 2 * i + g + 1)
                        e = per_head(eac, t, g, dr)
                        if dr == 0:
                            link(dve.tensor_tensor(heads(yt), heads(ps[:, g, :]), e, ALU.mult))
                            link(dve.tensor_tensor(heads(tmp[:, :]), heads(xs[:, t, sl]), skip[:, H8 * g:H8 * (g + 1)].unsqueeze(
                                2).to_broadcast([P, H8, HD]), ALU.mult))
                            dve.tensor_tensor(yt, yt, tmp[:, :], ALU.add).then_inc(y_out, 1)
                        else:
                            if 2 * i + g:
                                dve.wait_ge(y_out, 2 * i + g)
                            link(dve.tensor_tensor(heads(tmp[:, :]), heads(ps[:, g, :]), e, ALU.mult))
                            dve.tensor_tensor(yt, yt, tmp[:, :], ALU.add).then_inc(y_out, 1)
                for g in range(2):
                    sl = slice(g * HALF, (g + 1) * HALF)
                    s0, s1 = S[u % 2][:, sl], S[(u + 1) % 2][:, sl]
                    link(dve.tensor_tensor(heads(s1), heads(s0), per_head(tot, t, g, dr), ALU.mult))
                    dve.wait_ge(inc_ready, 2 * u + g + 1)
                    dve.tensor_tensor(s1, ps[:, 2 + g, :], s1, ALU.add).then_inc(state_out, 1)
                if dr == 0 and t >= CT_:
                    for g in range(2):
                        sl = slice(g * HALF, (g + 1) * HALF)
                        j = 2 * i + g
                        dve.wait_ge(cb_ready, j + 1)
                        for w in range(2):
                            ins = dve.tensor_tensor(cb[:, w, :], ps[:, 4, 0:P], tri[:, w, :], ALU.mult)
                        ins.then_inc(cb_out, 1)
                        dve.wait_ge(cb_out, j + 1)

                        def cap(m):
                            w, q = divmod(m, 2)
                            nq = quad(i, g, w, q)
                            dve.wait_ge(a_ready, nq + 1)
                            if nq >= 2:
                                dve.wait_ge(diag_done, nq - 1)
                            for h in range(4):
                                c = 16 * w + H8 * g + 4 * q + h
                                ins = dve.tensor_scalar(E[nq % 2][:, h, :], ps[:, 5 + nq % 2, h * P:(h + 1) * P],
                                                        ac[:, t, c:c + 1], 0.0, ALU.subtract, ALU.min)
                            ins.then_inc(capped, 1)

                        def mask(m):
                            w, q = divmod(m, 2)
                            nq = quad(i, g, w, q)
                            dve.wait_ge(exped, nq + 1)
                            e = E[nq % 2][:, :, :]
                            dve.tensor_tensor(e, e, cb[:, w, :].unsqueeze(1).to_broadcast([P, 4, P]),
                                              ALU.mult).then_inc(w_ready, 1)

                        cap(0)
                        cap(1)
                        mask(0)
                        cap(2)
                        mask(1)
                        cap(3)
                        mask(2)
                        mask(3)
                        dve.wait_ge(diag_done, 4 * (j + 1))
                        yt = y[:, t - CT_, sl]
                        dve.wait_ge(y_out, 4 * i + 2 + g)
                        dve.tensor_tensor(yt, ps[:, 7, :], yt, ALU.add).then_inc(y_out, 1)
                dve.wait_ge(state_out, 2 * u + 4)

        @block.scalar
        def _(act):
            if dr == 0:
                for m in range(len(lat_units) * 8):
                    act.wait_ge(capped, m + 1)
                    act.activation(E[m % 2][:, :, :], E[m % 2][:, :, :], ACT.Exp).then_inc(exped, 1)
    k.done(sems)


def ffn_up(k, XT, G, lay):
    nc, ws, ps, d = k.nc, k.ws, k.ps, k.d
    taps = lay("taps", [P, 4, KF])
    g_raw = [lay(f"gate{i}", [P, LAT + 2]) for i in range(2)]
    act_t = [lay(f"conv{i}", [P, LAT]) for i in range(2)]
    chunks = ws.take(KF)
    gate_ready, value_ready = {}, {}
    for jj in range(KF // 2):
        for which in range(2):
            for i in range(2):
                ws.count += 1
                (gate_ready, value_ready)[which][2 * jj + i] = ws.count
            ws.end[chunks[2 * jj + which]] = ws.count
    (taps_in, padded, gate_out, chain, convolved, activated, done) = sems = k.sems(
        "taps_in", "padded", "gate_out", "dve_chain", "convolved", "activated", "done")

    def wide(j, which):
        b = 4 * (j % 2) + 2 * which
        return ps[:, b:b + 2, :].rearrange("p a b -> p (a b)")

    with nc.Block() as block:
        @block.sync
        def _(sp):
            for i in range(3):
                sp.dma_start(taps[:, i, :], d["ffn_conv_w_2"][0, i].rearrange("(c p) -> p c", p=P)).then_inc(taps_in, 16)
            sp.dma_start(taps[:, 3, :], d["ffn_conv_b_2"][0].rearrange("(c p) -> p c", p=P)).then_inc(taps_in, 16)
            ws.load_until(sp, ws.taken)

        @block.tensor
        def _(pe):
            for jj in range(KF // 2):
                for which in range(2):
                    c = chunks[2 * jj + which]
                    ws.wait(pe, c)
                    for i in range(2):
                        j = 2 * jj + i
                        if j >= 2:
                            pe.wait_ge(*((gate_out, j - 1), (done, j - 1))[which])
                        for b in range(2):
                            for kk in range(KD):
                                mm = pe.matmul(ps[:, 4 * (j % 2) + 2 * which + b, :], ws.tile(c)[:, kk, i * P:(i + 1) * P],
                                               XT[:, kk, CTX + b * HALF:CTX + (b + 1) * HALF],
                                               start=(kk == 0), stop=(kk == KD - 1))
                        mm.then_inc(ws.products, 1)

        @block.gpsimd
        def _(pool):
            for i in range(2):
                pool.memset(g_raw[i][:, 0:1], 0.0)
                pool.memset(g_raw[i][:, LAT + 1:LAT + 2], 0.0).then_inc(padded, 1)

        @block.scalar
        def _(act):
            def gate(j):
                act.wait_ge(ws.products, gate_ready[j])
                if j >= 2:
                    act.wait_ge(convolved, j - 1)
                act.copy(g_raw[j % 2][:, 1:LAT + 1], wide(j, 0)).then_inc(gate_out, 1)

            gate(0)
            for j in range(KF):
                if j + 1 < KF:
                    gate(j + 1)
                act.wait_ge(convolved, j + 1)
                act.activation(act_t[j % 2][:, :], act_t[j % 2][:, :], ACT.Gelu).then_inc(activated, 1)

        @block.vector
        def _(dve):
            n = [0]

            def link(ins):
                ins.then_inc(chain, 1)
                n[0] += 1
                dve.wait_ge(chain, n[0])

            def conv(j):
                g, t = g_raw[j % 2], act_t[j % 2][:, :]
                dve.wait_ge(gate_out, j + 1)
                link(dve.tensor_scalar(t, g[:, 1:LAT + 1], taps[:, 1, j:j + 1], taps[:, 3, j:j + 1], ALU.mult, ALU.add))
                link(dve.scalar_tensor_tensor(t, g[:, 0:LAT], taps[:, 0, j:j + 1], t, ALU.mult, ALU.add))
                dve.scalar_tensor_tensor(t, g[:, 2:LAT + 2], taps[:, 2, j:j + 1], t, ALU.mult, ALU.add
                                         ).then_inc(convolved, 1)

            def times(j):
                dve.wait_ge(activated, j + 1)
                dve.wait_ge(ws.products, value_ready[j])
                dve.tensor_tensor(G(j), wide(j, 1), act_t[j % 2][:, :], ALU.mult).then_inc(done, 1)
                dve.wait_ge(done, j + 1)

            dve.wait_ge(taps_in, 64)
            dve.wait_ge(padded, 2)
            for j in range(KF):
                conv(j)
                if j >= 1:
                    times(j - 1)
            times(KF - 1)
    k.done(sems)


def first(k):
    (in_,) = sems = k.sems("identity_in")
    with k.nc.Block() as block:
        @block.sync
        def _(sp):
            sp.dma_start(k.ident[:, :], k.d["ident"]).then_inc(in_, 16)
            sp.wait_ge(in_, 16)
    k.done(sems)


def checkpoint(k, n):
    pass


def build_program(nc, d, out):
    k = K(nc, d, out)
    k.base = (nc.sbuf_base + 31) // 32 * 32
    with ExitStack() as ctx:
        k.ps = ctx.enter_context(nc.psum_tensor("ps", [P, 8, HALF], F32))
        k.ident = k.at("ident", [P, P], A_C)
        k.ws = WeightStream(k, weight_plan(d))
        k.out_stored = k.sems("out_stored0", "out_stored1", "out_stored2")
        k.buf = [k.at("buf_a", [P, KD, T], A_A), k.at("buf_b", [P, KD, T], A_B)]
        scratch = lambda: Layout(k, A_R, A_C)
        ctx.enter_context(nc.allow_non_contiguous_dma(reason="vectors of 1024 laid out over the partitions"))
        first(k)
        modulation(k)

        def rows(name, t):
            a = d[name]
            a = a[0] if len(a.shape) == 3 else a
            t0 = t if name.startswith("ctx") else t - CT_
            return a[t0 * P:(t0 + 1) * P, :]

        def tile(t, src, res=False, store=None, yt=None):
            return dict(t=t, stream=int(t < CT_), src=rows(src, t), res=res, yt=t if yt is None else yt,
                        store=rows(store, t) if store else None)

        XA, XB = k.buf
        normalize(k, [tile(t, "ctx" if t < CT_ else "x") for t in range(NT)], XA, (0, D), d["norm_g"][0], scratch())
        y = mixer_layer(k, 0, XA, XB)
        checkpoint(k, 1)
        normalize(k, [tile(t, "ctx" if t < CT_ else "x", res=True, store=None if t < CT_ else "h1") for t in range(NT)],
                  XB, (3 * D, 4 * D), d["norm_g"][1], scratch(), y=y, gates=2 * D)
        y = mixer_layer(k, 1, XB, XA)
        normalize(k, [tile(t, "ctx_2") if t < CT_ else tile(t, "h1", res=True, store="x2") for t in range(NT)],
                  XA, (M2, M2 + D), d["mix_pre_norm_2"][0], scratch(), y=y, gates=5 * D, pre=d["final_g"])
        second_block(k, XA, rows, tile)


def second_block(k, XA, rows, tile):
    nc, d = k.nc, k.d
    lat_tiles = [(t * P, P) for t in range(CT_, NT)]
    all_tiles = [(t * P, P) for t in range(NT)]

    def x(kx, t0, tn):
        return XA[:, kx, t0:t0 + tn]

    lay = Layout(k, A_R, A_C)
    tail = lambda: Layout(k, A_B + 32 * 1024, A_R)
    attnT = k.at("attn_t", [P, KD, LAT], A_B)
    qr = lay("qr", [P, 4, LAT])
    cqT, ckvT, krT = lay("cq_t", [P, 3, LAT]), lay("ckv_t", [P, 2, T]), lay("kr_t", [P, T])
    after = lay.o
    raw = lay("raw", [P, NT, O2_Z])
    project(k, [dict(mode="tm", x=x, kt=KD, cols=n, toks=all_tiles, do="copy",
                     dst=lambda s, t, o=o, n=n: raw[:, t, o:o + n]) for o, n in ((0, HALF), (HALF, O2_Z - HALF))])
    latents_prepare(k, raw, cqT, ckvT, krT, lay, tail())
    query_rope(k, cqT, qr, Layout(k, after, A_C), tail())
    lay = Layout(k, after, A_C)
    Kt = [lay(f"kt{i}", [P, T]) for i in range(2)]
    Q = [lay(f"q{i}", [P, LAT]) for i in range(2)]
    V = lay("v", [P, NT, 3 * HD])
    end = lay.o
    lw = tail()
    wts = [lw("wq", [P, 3, P]), lw("wk", [P, 2, P]), lw("wv", [P, 2, P])]
    for p in range(NH2 // 2):
        pair_projections(k, p, cqT, ckvT, krT, qr, Q, Kt, V, wts)
        units = []
        for odd in range(2):
            for b in range(2):
                units.append(dict(
                    rows=(0, P) if odd else (0, 96), rows_max=(0, P) if odd else (0, 97), row=32 if odd else 96,
                    odd=odd, nq=HALF, nk=T, q=Q[odd][:, b * HALF:(b + 1) * HALF], k=Kt[odd][:, :],
                    v=(lambda i, odd=odd: V[:, i, odd * HD:odd * HD + P]),
                    out=attnT[odd * HD:(odd + 1) * HD, p, b * HALF:(b + 1) * HALF]))
        attention(k, units, Layout(k, end, A_C), 96 ** -0.5, False)

    z = k.at("z", [P, LAT // P, D], A_R)
    project(k, [dict(mode="tm", x=x, kt=KD, cols=HALF, toks=lat_tiles, do="silu",
                     dst=lambda s, t, b=b: z[:, t, b * HALF:(b + 1) * HALF]) for b in range(2)])
    spill(k, [(d["attn"].rearrange("(c p) t -> p c t", p=P), attnT[:, :, :]),
              (d["z"].rearrange("(t p) n -> p t n", p=P), z[:, :, :])])
    lay = Layout(k, A_R, A_C)
    xs = lay("xs", [P, NT, D])
    bt, ct, btm = lay("bt", [P, 2, T]), lay("ct", [P, 2, T]), lay("btm", [P, NT, 2 * P])
    taps_lay = lay.o
    raw, conv = k.at("xbc_raw", [P, 4, T], A_B), k.at("xbc_conv", [P, 4, T], A_B + 4 * T * 4)
    for j0 in range(0, 12, 4):
        project(k, [dict(mode="fm", x=x, kt=KD, cols=HALF, toks=ALL_BLOCKS, do="copy",
                         dst=lambda s, n: raw[:, s, ALL_BLOCKS[n][0]:ALL_BLOCKS[n][0] + ALL_BLOCKS[n][1]])])
        ssd_conv(k, j0, raw, conv, xs, bt, ct, btm, Layout(k, taps_lay, A_C))
    skip = lay("skip", [P, NH2])
    layb = Layout(k, A_B, A_R)
    dt, w_end, tot, eac, ac, dta = (layb(n, [P, NT, ND]) for n in ("dt", "w_end", "tot", "eac", "ac", "dta"))
    tri = layb("tri", [P, 2, P])
    project(k, [dict(mode="tm", x=x, kt=KD, cols=ND, toks=all_tiles, do="copy", dst=lambda s, t: dt[:, t, :])])
    ssd_decays(k, dt, w_end, tot, eac, ac, dta, tri, skip, Layout(k, layb.o, A_R))
    y = k.at("ssd_y", [P, LAT // P, D], A_A)
    for direction in range(2):
        ssd_scan(k, direction, xs, bt, ct, btm, dt, dta, tri, w_end, tot, eac, ac, y, skip, Layout(k, layb.o, A_R))
    ssdT = k.at("ssd_t", [P, KD, T], A_R)
    lay = Layout(k, A_R + KD * T * 4, A_C)
    normalize(k, [dict(t=t, stream=0, src=d["z"][(t - CT_) * P:(t - CT_ + 1) * P, :], res=True, yt=t - CT_, store=None)
                  for t in range(CT_, NT)], ssdT, None, d["ssd_norm_2"][0], lay, y=y, gates=None)
    spill(k, [(attnT[:, :, :], d["attn"].rearrange("(c p) t -> p c t", p=P))])
    mix = k.at("mix", [P, LAT // P, D], A_A)
    project(k, [dict(mode="tm", kt=2 * KD, cols=HALF, toks=[(t * P, P) for t in range(LAT // P)], do="copy",
                     x=lambda kx, t0, tn: (attnT[:, kx, t0:t0 + tn] if kx < KD else
                                           ssdT[:, kx - KD, CTX + t0:CTX + t0 + tn]),
                     dst=lambda s, t, b=b: mix[:, t, b * HALF:(b + 1) * HALF]) for b in range(2)])

    X2 = k.buf[1]
    normalize(k, [tile(t, "x2", res=True, store="x3", yt=t - CT_) for t in range(CT_, NT)], X2,
              (M2 + 3 * D, M2 + 4 * D), d["ffn_pre_norm_2"][0], Layout(k, A_R, A_C), y=mix, gates=M2 + 2 * D,
              post=d["mix_post_norm_2"][0])
    GA = KD + 1
    g_a = k.at("g_a", [P, GA, LAT], A_A)
    lay = Layout(k, A_R, A_C)
    g_r = lay("g_r", [P, KF - GA, LAT])
    G = lambda j: g_a[:, j, :] if j < GA else g_r[:, j - GA, :]
    ffn_up(k, X2, G, lay)
    down = k.at("down", [P, LAT // P, D], A_B)
    project(k, [dict(mode="tm", kt=KF, cols=HALF, toks=[(t * P, P) for t in range(LAT // P)], do="copy",
                     x=lambda kx, t0, tn: G(kx)[:, t0:t0 + tn],
                     dst=lambda s, t, b=b: down[:, t, b * HALF:(b + 1) * HALF]) for b in range(2)])
    final = []
    for t in range(CT_, NT):
        w = tile(t, "x3", res=True, yt=t - CT_)
        w["store"] = k.out[0, (t - CT_) * P:(t - CT_ + 1) * P, :]
        final.append(w)
    normalize(k, final, None, None, None, Layout(k, A_R, A_C), y=down, gates=M2 + 5 * D,
              post=d["ffn_post_norm_2"][0], stored=k.out_stored)



def constants():
    r = np.arange(P)
    tri = np.stack([r[:, None] <= r[None, :], r[:, None] >= r[None, :]], 1).astype(np.float32)
    masks = np.zeros((2, P, NL + 1, P), np.float32)
    s, t = r[:, None], r[None, :]
    for l, h in enumerate(LEVELS):
        same = s // (2 * h) == t // (2 * h)
        masks[0, :, l] = same & (s % (2 * h) < h) & (t % (2 * h) >= h)
        masks[1, :, l] = same & (s % (2 * h) >= h) & (t % (2 * h) < h)
    masks[:, :, NL] = s == t

    def dft(n, scale):
        a = np.arange(n, dtype=np.int64)
        w = 2 * np.pi * ((a[:, None] * a[None, :]) % n) / n
        return np.cos(w) * scale, np.sin(w) * scale

    def positions(n):
        return [np.concatenate(dft(n, n ** -0.5)).astype(np.float32)]

    c, sn = dft(HD, HD ** -0.5)
    ch = np.zeros((P, 2, P))
    for g in range(2):
        ch[g * HD:(g + 1) * HD, 0, g * HD:(g + 1) * HD] = c
        ch[g * HD:(g + 1) * HD, 1, g * HD:(g + 1) * HD] = -sn
    row, col = np.arange(LAT) // 64, np.arange(LAT) % 64
    f1 = (np.float32(10000.0) ** (-np.arange(16, dtype=np.float32) / np.float32(16))).astype(np.float32)
    row, col = row.astype(np.float32), col.astype(np.float32)
    ang = np.concatenate([row[:, None] * f1, col[:, None] * f1], 1)
    f2 = (np.float32(10000.0) ** (-np.arange(0, 16, 2, dtype=np.float32) / np.float32(16))).astype(np.float32)
    ar, acl = row[:, None] * f2, col[:, None] * f2
    ang2 = np.concatenate([ar, ar, acl, acl], 1)
    sign = np.tile(np.repeat(np.array([-1.0, 1.0], np.float32), 8), 2)
    r2 = np.stack([np.cos(ang2), np.sin(ang2) * sign]).astype(np.float32)
    return dict(
        ident=np.eye(P, dtype=np.float32), tri=tri, level_masks=masks, dft_channels=ch.astype(np.float32),
        dft_ctx=positions(CTX)[0], dft_lat=positions(LAT)[0],
        rope1=np.stack([np.cos(ang), np.sin(ang)]).astype(np.float32),
        rope2_tm=r2, rope2_fm=np.ascontiguousarray(np.tile(r2.transpose(0, 2, 1), (1, 4, 1))))


def layouts(inputs):
    wq = np.asarray(inputs["w_q_up_2"])[0].reshape(QL, NH2, NOPE + RD)
    wkv = np.asarray(inputs["w_kv_up_2"])[0].reshape(KVL, NH2, NOPE + HD)
    rope = wq[:, :, NOPE:]
    swap = np.concatenate([np.arange(8, 16), np.arange(8), np.arange(24, 32), np.arange(16, 24)])
    c = np.ascontiguousarray
    return dict(wq_nope=c(wq[:, :, :NOPE]).reshape(QL, -1), wq_rope=c(rope).reshape(QL, -1),
                wq_rope_sw=c(rope[:, :, swap]).reshape(QL, -1), wk_nope=c(wkv[:, :, :NOPE]).reshape(KVL, -1),
                wv=c(wkv[:, :, NOPE:]).reshape(KVL, -1))


SCRATCH = {"mod": [2, NMOD], "h1": [LAT, D], "x2": [LAT, D], "x3": [LAT, D], "attn": [D, LAT], "z": [LAT, D]}


def kernel(**inputs):
    import concourse.bacc as bacc
    from concourse.bass_utils import run_bass_kernel_spmd

    nc = bacc.Bacc("TRN2", target_bir_lowering=False, num_devices=1)
    arrays = {n: np.ascontiguousarray(a) for n, a in inputs.items() if n not in ("w_q_up_2", "w_kv_up_2")}
    arrays.update(layouts(inputs))
    arrays.update(constants())
    d = {n: nc.dram_tensor(f"in_{n}", a.shape, mybir.dt.from_np(a.dtype), kind="ExternalInput").ap()
         for n, a in arrays.items()}
    for n, shape in SCRATCH.items():
        d[n] = nc.dram_tensor(f"scratch_{n}", shape, F32, kind="Internal").ap()
    out = nc.dram_tensor("out", [1, LAT, D], F32, kind="ExternalOutput").ap()
    build_program(nc, d, out)
    r = run_bass_kernel_spmd(nc, [{f"in_{n}": a for n, a in arrays.items()}], core_ids=[0])
    return r.results[0]["out"]
```
